# Optimizing a Trainium2 kernel written in Bass

```python
import math
import jax, jax.numpy as jnp
from jax import lax
import numpy as np

D_MODEL = 1024
BATCH = 1
SEQ = 1024
DEPTH = 1

GDN_HEADS = 4
GDN_HEAD_DIM = 128
GDN_WIDTH = GDN_HEADS * GDN_HEAD_DIM
CONV_WIDTH = 4
CHUNK = 64
SWA_HEADS = 8
SWA_HEAD_DIM = 64
SWA_WIDTH = SWA_HEADS * SWA_HEAD_DIM
DILATED_PATTERNS = ((128, 1), (512, 4), (2048, 16))
NUM_BUCKETS = 32
MAX_DISTANCE = 2048
MIX_WIDTH = GDN_WIDTH + SWA_WIDTH
IN_SIZES = (GDN_WIDTH, GDN_WIDTH, GDN_WIDTH, GDN_WIDTH, GDN_HEADS, GDN_HEADS,
            SWA_WIDTH, SWA_WIDTH, SWA_WIDTH)
IN_COLS = sum(IN_SIZES)
D_FF = ((-(-8 * D_MODEL // 3)) + 255) // 256 * 256
RMS_EPS = 1e-6


def rmsnorm(x, g):
    xf = x.astype(jnp.float32)
    y = xf * lax.rsqrt(jnp.mean(xf * xf, axis=-1, keepdims=True) + RMS_EPS)
    return (y * g.astype(jnp.float32)).astype(x.dtype)

def l2norm(x):
    return x * lax.rsqrt(jnp.sum(x * x, axis=-1, keepdims=True) + 1e-6)

def causal_depthwise_conv(x, w):
    K, C = w.shape
    return lax.conv_general_dilated(x, w[:, None, :].astype(x.dtype), (1,), ((K - 1, 0),),
                                    dimension_numbers=('NWC', 'WIO', 'NWC'),
                                    feature_group_count=C)

def chunk_gated_delta_rule(q, k, v, g, beta):
    Bn, S, H, Dk = q.shape
    Dv = v.shape[-1]
    N = S // CHUNK

    def chunks(t):
        t = t.reshape((Bn, N, CHUNK, H) + t.shape[3:])
        return jnp.moveaxis(jnp.moveaxis(t, 1, 0), 3, 2)

    qc, kc, vc = chunks(q), chunks(k), chunks(v)
    bc = chunks(beta)
    gc = jnp.cumsum(chunks(g), axis=-1)
    idx = jnp.arange(CHUNK)
    causal = idx[:, None] >= idx[None, :]
    strict = idx[:, None] > idx[None, :]
    decay = jnp.exp(jnp.where(causal, gc[..., :, None] - gc[..., None, :], -jnp.inf))
    kb = kc * bc[..., None]
    a = jnp.where(strict, jnp.einsum('nbhid,nbhjd->nbhij', kb, kc) * decay, 0.0)
    eye = jnp.eye(CHUNK, dtype=q.dtype)
    t_inv = lax.linalg.triangular_solve(eye + a, jnp.broadcast_to(eye, a.shape),
                                        left_side=True, lower=True)
    u = t_inv @ (vc * bc[..., None])
    w = t_inv @ (kb * jnp.exp(gc)[..., None])
    attn = jnp.einsum('nbhid,nbhjd->nbhij', qc, kc) * decay
    q_dec = qc * jnp.exp(gc)[..., None]
    k_dec = kc * jnp.exp(gc[..., -1:] - gc)[..., None]
    g_end = jnp.exp(gc[..., -1])

    def step(state, inp):
        u_i, w_i, attn_i, qd_i, kd_i, ge_i = inp
        v_new = u_i - jnp.einsum('bhck,bhkv->bhcv', w_i, state)
        o_i = (jnp.einsum('bhck,bhkv->bhcv', qd_i, state)
               + jnp.einsum('bhij,bhjv->bhiv', attn_i, v_new))
        state = state * ge_i[..., None, None] + jnp.einsum('bhck,bhcv->bhkv', kd_i, v_new)
        return state, o_i

    s0 = jnp.zeros((Bn, H, Dk, Dv), q.dtype)
    _, o = lax.scan(step, s0, (u, w, attn, q_dec, k_dec, g_end))
    return jnp.moveaxis(o, 0, 1).transpose(0, 1, 3, 2, 4).reshape(Bn, S, H, Dv)

def gated_deltanet(q, k, v, gate, beta_logit, a_logit, conv_w, a_log, dt_bias, onorm_g):
    f32 = jnp.float32
    Bn, S, _ = q.shape
    qkv = jax.nn.silu(causal_depthwise_conv(jnp.concatenate([q, k, v], axis=-1), conv_w)).astype(f32)
    q, k, v = jnp.split(qkv, 3, axis=-1)
    heads = lambda t: t.reshape(Bn, S, GDN_HEADS, GDN_HEAD_DIM)
    q = l2norm(heads(q)) * GDN_HEAD_DIM ** -0.5
    k = l2norm(heads(k))
    v = heads(v)
    beta = jax.nn.sigmoid(beta_logit.astype(f32))
    g = -jnp.exp(a_log.astype(f32)) * jax.nn.softplus(a_logit.astype(f32) + dt_bias.astype(f32))
    o = chunk_gated_delta_rule(q, k, v, g, beta)
    o = o * lax.rsqrt(jnp.mean(o * o, axis=-1, keepdims=True) + RMS_EPS) * onorm_g.astype(f32)
    o = o * jax.nn.silu(heads(gate).astype(f32))
    return o.reshape(Bn, S, GDN_WIDTH).astype(gate.dtype)

def t5_causal_bucket(dist):
    max_exact = NUM_BUCKETS // 2
    d = jnp.maximum(dist, 1).astype(jnp.float32)
    log_b = max_exact + (jnp.log(d / max_exact) / math.log(MAX_DISTANCE / max_exact)
                         * (NUM_BUCKETS - max_exact)).astype(jnp.int32)
    return jnp.where(dist < max_exact, dist, jnp.minimum(log_b, NUM_BUCKETS - 1))

def dilated_band(q, k, v, rel_bias, window, dilation):
    Bn, S, H, Dh = q.shape
    w = window // dilation
    L = S // dilation
    nb = -(-L // w)
    Lp = nb * w

    def to_sub(t):
        t = t.reshape(Bn, L, dilation, H, Dh).transpose(0, 3, 2, 1, 4)
        return jnp.pad(t, ((0, 0), (0, 0), (0, 0), (0, Lp - L), (0, 0)))

    blocks = lambda t: t.reshape(Bn, H, dilation, nb, w, Dh)

    def band(t):
        prev = jnp.pad(t, ((0, 0), (0, 0), (0, 0), (w, 0), (0, 0)))[:, :, :, :Lp]
        return jnp.concatenate([blocks(prev), blocks(t)], axis=-2)

    qb, kb, vb = blocks(to_sub(q)), band(to_sub(k)), band(to_sub(v))
    qi = jnp.arange(w)[:, None]
    kj = jnp.arange(2 * w)[None, :]
    rel = qi + w - kj
    blk = jnp.arange(nb)[:, None, None]
    valid = (rel >= 0) & (rel <= w) & (blk * w + kj - w >= 0)
    bias_steps = rel_bias[t5_causal_bucket(jnp.arange(w + 1) * dilation)]
    bias = jnp.moveaxis(bias_steps[jnp.clip(rel, 0, w)], -1, 0).astype(jnp.float32)
    logits = jnp.einsum('bhrnqd,bhrnkd->bhrnqk', qb, kb) * Dh ** -0.5 + bias[None, :, None, None]
    logits = jnp.where(valid, logits, -jnp.inf)
    m = jnp.max(logits, axis=-1)
    p = jnp.exp(logits - m[..., None])
    s = jnp.sum(p, axis=-1)
    num = jnp.einsum('bhrnqk,bhrnkd->bhrnqd', p, vb)

    def from_sub(t):
        rest = t.shape[5:]
        t = t.reshape((Bn, H, dilation, Lp) + rest)[:, :, :, :L]
        t = t.transpose((0, 3, 2, 1) + tuple(range(4, t.ndim)))
        return t.reshape((Bn, S, H) + rest)

    return from_sub(num), from_sub(m), from_sub(s)

def dilated_attention(q, k, v, rel_bias):
    Bn, S, _ = q.shape
    heads = lambda t: t.reshape(Bn, S, SWA_HEADS, SWA_HEAD_DIM).astype(jnp.float32)
    qh, kh, vh = heads(q), heads(k), heads(v)
    parts = [dilated_band(qh, kh, vh, rel_bias, win, dil) for win, dil in DILATED_PATTERNS]
    nums = jnp.stack([pt[0] for pt in parts])
    ms = jnp.stack([pt[1] for pt in parts])
    ss = jnp.stack([pt[2] for pt in parts])
    wts = jnp.exp(ms - jnp.max(ms, axis=0, keepdims=True))
    out = jnp.sum(wts[..., None] * nums, axis=0) / jnp.sum(wts * ss, axis=0)[..., None]
    return out.reshape(Bn, S, SWA_WIDTH).astype(q.dtype)

def first_inputs(seed: int = 0) -> dict:
    key = jax.random.key(seed)
    ks = jax.random.split(key, 16)
    f32 = jnp.float32
    nrm = lambda k_, shape, scale: jax.random.normal(k_, shape, f32) * scale
    dt = jnp.exp(jax.random.uniform(ks[4], (DEPTH, GDN_HEADS), f32, math.log(1e-3), math.log(1e-1)))
    return {
        'x': nrm(ks[0], (BATCH, SEQ, D_MODEL), 1.0),
        'w_in': nrm(ks[1], (DEPTH, D_MODEL, IN_COLS), D_MODEL ** -0.5),
        'conv_w': nrm(ks[2], (DEPTH, CONV_WIDTH, 3 * GDN_WIDTH), CONV_WIDTH ** -0.5),
        'a_log': jnp.log(jax.random.uniform(ks[3], (DEPTH, GDN_HEADS), f32, 1.0, 16.0)),
        'dt_bias': dt + jnp.log(-jnp.expm1(-dt)),
        'onorm_g': 1.0 + nrm(ks[5], (DEPTH, GDN_HEAD_DIM), 0.1),
        'rel_bias': nrm(ks[6], (NUM_BUCKETS, SWA_HEADS), 0.2),
        'w_out': nrm(ks[7], (DEPTH, MIX_WIDTH, D_MODEL), MIX_WIDTH ** -0.5),
        'g_mix_pre': 1.0 + nrm(ks[8], (DEPTH, D_MODEL), 0.1),
        'g_mix_post': 1.0 + nrm(ks[9], (DEPTH, D_MODEL), 0.1),
        'w_gate': nrm(ks[10], (DEPTH, D_MODEL, D_FF), D_MODEL ** -0.5),
        'w_up': nrm(ks[11], (DEPTH, D_MODEL, D_FF), D_MODEL ** -0.5),
        'w_down': nrm(ks[12], (DEPTH, D_FF, D_MODEL), D_FF ** -0.5),
        'g_ffn_pre': 1.0 + nrm(ks[13], (DEPTH, D_MODEL), 0.1),
        'g_ffn_post': 1.0 + nrm(ks[14], (DEPTH, D_MODEL), 0.1),
    }

def first_block(x, w_in, conv_w, a_log, dt_bias, onorm_g, rel_bias, w_out, g_mix_pre, g_mix_post,
              w_gate, w_up, w_down, g_ffn_pre, g_ffn_post):
    split_at = [int(c) for c in np.cumsum(IN_SIZES)[:-1]]
    for l in range(DEPTH):
        h = rmsnorm(x, g_mix_pre[l])
        proj = h @ w_in[l]
        qa, ka, va, gate_a, beta_a, alpha_a, qb, kb, vb = jnp.split(proj, split_at, axis=-1)
        out_a = gated_deltanet(qa, ka, va, gate_a, beta_a, alpha_a,
                               conv_w[l], a_log[l], dt_bias[l], onorm_g[l])
        out_b = dilated_attention(qb, kb, vb, rel_bias)
        mix = jnp.concatenate([out_a, out_b], axis=-1) @ w_out[l]
        x = x + rmsnorm(mix, g_mix_post[l])
        h = rmsnorm(x, g_ffn_pre[l])
        f = (jax.nn.silu(h @ w_gate[l]) * (h @ w_up[l])) @ w_down[l]
        x = x + rmsnorm(f, g_ffn_post[l])
    return x


DEPTH_2 = 2

GRID_W = 64
CTX_LEN = 256
HEAD_DIM = 64
RWKV_HEADS = 6
GQA_Q_HEADS = 6
GQA_KV_HEADS = 2
GQA_REP = GQA_Q_HEADS // GQA_KV_HEADS
NA_HEADS = 4
RWKV_W = RWKV_HEADS * HEAD_DIM
GQA_W = GQA_Q_HEADS * HEAD_DIM
GQA_KV_W = GQA_KV_HEADS * HEAD_DIM
NA_W = NA_HEADS * HEAD_DIM
D_MIX = RWKV_W + GQA_W + NA_W
DECAY_RANK = 32
ICLR_RANK = 32
RWKV_CONV_W = 3 * RWKV_W + 2 * DECAY_RANK + 2 * ICLR_RANK
RWKV_SPLIT = (RWKV_W, 2 * RWKV_W, 3 * RWKV_W, 3 * RWKV_W + 2 * DECAY_RANK)
_SPLIT_SIZES = (RWKV_CONV_W, RWKV_W, GQA_W, GQA_KV_W, GQA_KV_W, GQA_W, NA_W, NA_W, NA_W, NA_W)
D_IN = sum(_SPLIT_SIZES)
SPLIT_POINTS = tuple(int(s) for s in np.cumsum(_SPLIT_SIZES)[:-1])
Q_BLOCK = 128
NA_WIN_ROWS = 8
NA_WIN_COLS = 16
ROPE_THETA = 10000.0
DEEPNORM_ALPHA = (2 * DEPTH_2) ** 0.25
DEEPNORM_BETA = (8 * DEPTH_2) ** -0.25
LN_EPS = 1e-5
GN_EPS = 64e-5


def _layer_norm(x, g, b):
    xf = x.astype(jnp.float32)
    mu = jnp.mean(xf, axis=-1, keepdims=True)
    var = jnp.mean(jnp.square(xf - mu), axis=-1, keepdims=True)
    return ((xf - mu) * lax.rsqrt(var + LN_EPS) * g + b).astype(x.dtype)

def _rms_norm(x, g):
    xf = x.astype(jnp.float32)
    return (xf * lax.rsqrt(jnp.mean(xf * xf, axis=-1, keepdims=True) + RMS_EPS) * g).astype(x.dtype)

def _centred_conv3(x, w):
    xp = jnp.pad(x, ((0, 0), (1, 1), (0, 0)))
    return w[0] * xp[:, :-2] + w[1] * xp[:, 1:-1] + w[2] * xp[:, 2:]

def _axial_rope_tables(n_tokens):
    t = jnp.arange(n_tokens, dtype=jnp.int32)
    row = (t // GRID_W).astype(jnp.float32)
    col = (t % GRID_W).astype(jnp.float32)
    n_freq = HEAD_DIM // 4
    inv_freq = ROPE_THETA ** (-jnp.arange(n_freq, dtype=jnp.float32) / n_freq)
    ang_r = row[:, None] * inv_freq
    ang_c = col[:, None] * inv_freq
    ang = jnp.concatenate([ang_r, ang_r, ang_c, ang_c], axis=-1)
    return jnp.cos(ang), jnp.sin(ang)

def _apply_axial_rope(x, cos, sin):
    x1, x2, x3, x4 = jnp.split(x, 4, axis=-1)
    rotated = jnp.concatenate([-x2, x1, -x4, x3], axis=-1)
    return (x * cos[:, None] + rotated * sin[:, None]).astype(x.dtype)

def _rwkv_inputs(u, conv_w, decay_w0, decay_w2, iclr_a0, iclr_a2, k_k, k_a):
    u = _centred_conv3(u, conv_w).astype(jnp.float32)
    B, T, _ = u.shape
    r, k, v, dd, ad = jnp.split(u, RWKV_SPLIT, axis=-1)
    dd = jnp.tanh(dd.reshape(B, T, 2, DECAY_RANK))
    ad = ad.reshape(B, T, 2, ICLR_RANK)
    w_log = -jax.nn.softplus(-(decay_w0 + jnp.einsum('btdr,drc->btdc', dd, decay_w2))) - 0.5
    decay = jnp.exp(-jnp.exp(w_log))
    iclr = jax.nn.sigmoid(iclr_a0 + jnp.einsum('btdr,drc->btdc', ad, iclr_a2))
    kk = (k * k_k).reshape(B, T, RWKV_HEADS, HEAD_DIM)
    kk = kk * lax.rsqrt(jnp.maximum(jnp.sum(kk * kk, axis=-1, keepdims=True), 1e-12))
    kk = kk.reshape(B, T, RWKV_W)
    kd = k[:, :, None] * (1.0 + (iclr - 1.0) * k_a)
    bd = kk[:, :, None] * iclr

    def heads_t(z):
        return jnp.moveaxis(z.reshape(z.shape[:-1] + (RWKV_HEADS, HEAD_DIM)), 1, 0)

    return (heads_t(r), heads_t(decay), heads_t(kd), heads_t(v), heads_t(kk), heads_t(bd))

def _rwkv7_step(S, inp):
    r, w, k, v, kk, b = inp
    sa = jnp.einsum('bhvk,bhk->bhv', S, kk)
    S = S * w[:, :, None, :] - sa[..., None] * b[:, :, None, :] + v[..., None] * k[:, :, None, :]
    return S, jnp.einsum('bhvk,bhk->bhv', S, r)

def _rwkv_bidir(rin, S0_f, S0_b):
    r, decay, kd, v, kk, bd = rin
    S_f, y_f = lax.scan(_rwkv7_step, S0_f, (r, decay[:, :, 0], kd[:, :, 0], v, kk, bd[:, :, 0]))
    S_b, y_b = lax.scan(_rwkv7_step, S0_b, (r, decay[:, :, 1], kd[:, :, 1], v, kk, bd[:, :, 1]),
                        reverse=True)
    return S_f, S_b, y_f + y_b

def _rwkv_output(ys, rin, r_k, gn_g, gn_b, dtype):
    r, _, kd, v, _, _ = rin
    T, B = ys.shape[:2]
    mu = jnp.mean(ys, axis=-1, keepdims=True)
    var = jnp.mean(jnp.square(ys - mu), axis=-1, keepdims=True)
    yn = ((ys - mu) * lax.rsqrt(var + GN_EPS)).reshape(T, B, RWKV_W) * gn_g + gn_b
    bonus = jnp.sum(jnp.sum(r[:, :, None] * kd * r_k, axis=-1, keepdims=True), axis=2) * v
    return jnp.moveaxis(yn + bonus.reshape(T, B, RWKV_W), 0, 1).astype(dtype)

def _block_attention(q, keys, vals):
    B, T, G, R, D = q.shape
    qb = jnp.moveaxis(q.reshape(B, T // Q_BLOCK, Q_BLOCK, G, R, D), 1, 0) * (D ** -0.5)

    def one_block(qi):
        s = jnp.einsum('bqgrd,bsgd->bgrqs', qi, keys).astype(jnp.float32)
        p = jax.nn.softmax(s, axis=-1).astype(vals.dtype)
        return jnp.einsum('bgrqs,bsgd->bqgrd', p, vals)

    o = lax.map(one_block, qb)
    return jnp.moveaxis(o, 0, 1).reshape(B, T, G * R * D)

def _neighbourhood_attention(q, k, v, k_ctx, v_ctx, rpb):
    B, L, H, D = q.shape
    rows = L // GRID_W
    win_r = min(NA_WIN_ROWS, rows)
    n_nb = win_r * NA_WIN_COLS
    qg = q.reshape(B, rows, GRID_W, H, D) * (D ** -0.5)
    kg = k.reshape(B, rows, GRID_W, H, D)
    vg = v.reshape(B, rows, GRID_W, H, D)
    cols = jnp.arange(GRID_W, dtype=jnp.int32)
    c_start = jnp.clip(cols - NA_WIN_COLS // 2, 0, GRID_W - NA_WIN_COLS)
    c_idx = c_start[:, None] + jnp.arange(NA_WIN_COLS, dtype=jnp.int32)[None, :]
    dc = c_idx - cols[:, None] + (NA_WIN_COLS - 1)

    def row_block(r):
        r_start = jnp.clip(r - win_r // 2, 0, rows - win_r)
        q_r = lax.dynamic_index_in_dim(qg, r, axis=1, keepdims=False)
        k_nb = lax.dynamic_slice_in_dim(kg, r_start, win_r, axis=1)[:, :, c_idx]
        v_nb = lax.dynamic_slice_in_dim(vg, r_start, win_r, axis=1)[:, :, c_idx]
        dr = r_start + jnp.arange(win_r, dtype=jnp.int32) - r + (NA_WIN_ROWS - 1)
        bias = rpb[:, dr[None, :, None], dc[:, None, :]]
        s_nb = jnp.einsum('bqhd,bpqjhd->bhqpj', q_r, k_nb).astype(jnp.float32) + bias
        s_ctx = jnp.einsum('bqhd,bchd->bhqc', q_r, k_ctx).astype(jnp.float32)
        s = jnp.concatenate([s_nb.reshape(B, H, GRID_W, n_nb), s_ctx], axis=-1)
        p = jax.nn.softmax(s, axis=-1).astype(v.dtype)
        p_nb = p[..., :n_nb].reshape(B, H, GRID_W, win_r, NA_WIN_COLS)
        return (jnp.einsum('bhqpj,bpqjhd->bqhd', p_nb, v_nb)
                + jnp.einsum('bhqc,bchd->bqhd', p[..., n_nb:], v_ctx))

    o = lax.map(row_block, jnp.arange(rows, dtype=jnp.int32))
    return jnp.moveaxis(o, 0, 1).reshape(B, L, H * D)

def _layer(x, ctx, c, c_ctx, rope, w_mod, b_mod, w_in, w_out, rwkv_conv, decay_w0, decay_w2,
           iclr_a0, iclr_a2, k_k, k_a, r_k, gn_g, gn_b, q_norm, k_norm, rpb, ln_g, ln_b, update_ctx):
    B, L, _ = x.shape
    cos, sin = rope
    shift, scale, gate = jnp.split(jax.nn.silu(c) @ w_mod + b_mod, 3, axis=-1)
    shift_c, scale_c, gate_c = jnp.split(jax.nn.silu(c_ctx) @ w_mod + b_mod, 3, axis=-1)
    h_lat = x * (1.0 + scale[:, None]) + shift[:, None]
    h_ctx = ctx * (1.0 + scale_c) + shift_c
    ru_l, rg_l, aq_l, ak_l, av_l, ag_l, nq_l, nk_l, nv_l, ng_l = jnp.split(h_lat @ w_in, SPLIT_POINTS, axis=-1)
    ru_c, rg_c, aq_c, ak_c, av_c, ag_c, nq_c, nk_c, nv_c, ng_c = jnp.split(h_ctx @ w_in, SPLIT_POINTS, axis=-1)

    rwkv_params = (rwkv_conv, decay_w0, decay_w2, iclr_a0, iclr_a2, k_k, k_a)
    rin_c = _rwkv_inputs(ru_c, *rwkv_params)
    rin_l = _rwkv_inputs(ru_l, *rwkv_params)
    S0 = jnp.zeros((B, RWKV_HEADS, HEAD_DIM, HEAD_DIM), jnp.float32)
    S_f, S_b, ys_c = _rwkv_bidir(rin_c, S0, S0)
    _, _, ys_l = _rwkv_bidir(rin_l, S_f, S_b)
    yr_l = _rwkv_output(ys_l, rin_l, r_k, gn_g, gn_b, x.dtype)

    def gqa_kv(kx, vx):
        T = kx.shape[1]
        return (_rms_norm(kx.reshape(B, T, GQA_KV_HEADS, HEAD_DIM), k_norm),
                vx.reshape(B, T, GQA_KV_HEADS, HEAD_DIM))

    def gqa_q(qx):
        return _rms_norm(qx.reshape(B, qx.shape[1], GQA_Q_HEADS, HEAD_DIM), q_norm)

    gk_l, gv_l = gqa_kv(ak_l, av_l)
    gk_l = _apply_axial_rope(gk_l, cos, sin)
    gq_l = _apply_axial_rope(gqa_q(aq_l), cos, sin)
    gk_c, gv_c = gqa_kv(ak_c, av_c)
    ya_l = _block_attention(gq_l.reshape(B, L, GQA_KV_HEADS, GQA_REP, HEAD_DIM),
                            jnp.concatenate([gk_c, gk_l], axis=1), jnp.concatenate([gv_c, gv_l], axis=1))

    def na_heads(u):
        return u.reshape(B, u.shape[1], NA_HEADS, HEAD_DIM)

    nk_c, nv_c = na_heads(nk_c), na_heads(nv_c)
    yn_l = _neighbourhood_attention(na_heads(nq_l), na_heads(nk_l), na_heads(nv_l), nk_c, nv_c, rpb)

    y_l = jnp.concatenate([yr_l * jax.nn.silu(rg_l), ya_l * jax.nn.silu(ag_l),
                           yn_l * jax.nn.silu(ng_l)], axis=-1) @ w_out
    x = _layer_norm(DEEPNORM_ALPHA * x + gate[:, None] * y_l, ln_g, ln_b)

    if update_ctx:
        n_ctx = ctx.shape[1]
        yr_c = _rwkv_output(ys_c, rin_c, r_k, gn_g, gn_b, ctx.dtype)
        ya_c = _block_attention(gqa_q(aq_c).reshape(B, n_ctx, GQA_KV_HEADS, GQA_REP, HEAD_DIM), gk_c, gv_c)
        yn_c = _block_attention(na_heads(nq_c)[:, :, :, None], nk_c, nv_c)
        y_c = jnp.concatenate([yr_c * jax.nn.silu(rg_c), ya_c * jax.nn.silu(ag_c),
                               yn_c * jax.nn.silu(ng_c)], axis=-1) @ w_out
        ctx = _layer_norm(DEEPNORM_ALPHA * ctx + gate_c * y_c, ln_g, ln_b)
    else:
        ctx = None
    return x, ctx

def second_inputs(seed: int = 0) -> dict:
    key = jax.random.key(seed)
    ks = jax.random.split(key, 24)

    def n(k, shape):
        return jax.random.normal(k, shape, jnp.float32)

    inv_d = D_MODEL ** -0.5
    return {
        'x': n(ks[0], (BATCH, SEQ, D_MODEL)),
        'c': n(ks[1], (BATCH, D_MODEL)),
        'ctx': n(ks[2], (BATCH, CTX_LEN, D_MODEL)),
        'c_ctx': n(ks[3], (D_MODEL,)),
        'w_mod': n(ks[4], (DEPTH_2, D_MODEL, 3 * D_MODEL)) * (0.5 * inv_d),
        'b_mod': 0.01 * n(ks[5], (DEPTH_2, 3 * D_MODEL)),
        'w_in': n(ks[6], (DEPTH_2, D_MODEL, D_IN)) * inv_d,
        'w_out': n(ks[7], (DEPTH_2, D_MIX, D_MODEL)) * (DEEPNORM_BETA * D_MIX ** -0.5),
        'rwkv_conv': jnp.array([0.25, 0.5, 0.25], jnp.float32)[None, :, None]
                     + 0.05 * n(ks[8], (DEPTH_2, 3, RWKV_CONV_W)),
        'decay_w0': n(ks[9], (DEPTH_2, 2, RWKV_W)),
        'decay_w2': 0.1 * n(ks[10], (DEPTH_2, 2, DECAY_RANK, RWKV_W)),
        'iclr_a0': 0.5 * n(ks[11], (DEPTH_2, 2, RWKV_W)),
        'iclr_a2': 0.1 * n(ks[12], (DEPTH_2, 2, ICLR_RANK, RWKV_W)),
        'rwkv_k_k': 0.85 + 0.05 * n(ks[13], (DEPTH_2, RWKV_W)),
        'rwkv_k_a': 1.0 + 0.05 * n(ks[14], (DEPTH_2, RWKV_W)),
        'rwkv_r_k': 0.1 * n(ks[15], (DEPTH_2, RWKV_HEADS, HEAD_DIM)),
        'rwkv_gn_g': 1.0 + 0.05 * n(ks[16], (DEPTH_2, RWKV_W)),
        'rwkv_gn_b': 0.01 * n(ks[17], (DEPTH_2, RWKV_W)),
        'gqa_q_norm': 1.0 + 0.05 * n(ks[18], (DEPTH_2, HEAD_DIM)),
        'gqa_k_norm': 1.0 + 0.05 * n(ks[19], (DEPTH_2, HEAD_DIM)),
        'na_rpb': 0.1 * n(ks[20], (DEPTH_2, NA_HEADS, 2 * NA_WIN_ROWS - 1, 2 * NA_WIN_COLS - 1)),
        'ln_g': 1.0 + 0.05 * n(ks[21], (DEPTH_2, D_MODEL)),
        'ln_b': 0.01 * n(ks[22], (DEPTH_2, D_MODEL)),
    }

def second_block(x, c, ctx, c_ctx, w_mod, b_mod, w_in, w_out, rwkv_conv, decay_w0, decay_w2,
              iclr_a0, iclr_a2, rwkv_k_k, rwkv_k_a, rwkv_r_k, rwkv_gn_g, rwkv_gn_b,
              gqa_q_norm, gqa_k_norm, na_rpb, ln_g, ln_b):
    rope = _axial_rope_tables(x.shape[1])
    for l in range(DEPTH_2):
        x, ctx = _layer(x, ctx, c, c_ctx, rope, w_mod[l], b_mod[l], w_in[l], w_out[l], rwkv_conv[l],
                        decay_w0[l], decay_w2[l], iclr_a0[l], iclr_a2[l], rwkv_k_k[l], rwkv_k_a[l],
                        rwkv_r_k[l], rwkv_gn_g[l], rwkv_gn_b[l], gqa_q_norm[l], gqa_k_norm[l],
                        na_rpb[l], ln_g[l], ln_b[l], l < DEPTH_2 - 1)
    return x


def setup_inputs(seed=0):
    out = dict(first_inputs(seed))
    for name, value in second_inputs(seed + 1).items():
        if name != "x":
            out[name + "_2"] = value
    return out


def reference(
    x, w_in, conv_w, a_log, dt_bias, onorm_g, rel_bias, w_out, g_mix_pre, g_mix_post, w_gate,
    w_up, w_down, g_ffn_pre, g_ffn_post, c_2, ctx_2, c_ctx_2, w_mod_2, b_mod_2, w_in_2, w_out_2,
    rwkv_conv_2, decay_w0_2, decay_w2_2, iclr_a0_2, iclr_a2_2, rwkv_k_k_2, rwkv_k_a_2,
    rwkv_r_k_2, rwkv_gn_g_2, rwkv_gn_b_2, gqa_q_norm_2, gqa_k_norm_2, na_rpb_2, ln_g_2, ln_b_2,
):
    x = first_block(
        x, w_in, conv_w, a_log, dt_bias, onorm_g, rel_bias, w_out, g_mix_pre, g_mix_post,
        w_gate, w_up, w_down, g_ffn_pre, g_ffn_post,
    )
    return second_block(
        x, c_2, ctx_2, c_ctx_2, w_mod_2, b_mod_2, w_in_2, w_out_2, rwkv_conv_2, decay_w0_2,
        decay_w2_2, iclr_a0_2, iclr_a2_2, rwkv_k_k_2, rwkv_k_a_2, rwkv_r_k_2, rwkv_gn_g_2,
        rwkv_gn_b_2, gqa_q_norm_2, gqa_k_norm_2, na_rpb_2, ln_g_2, ln_b_2,
    )


_drawn_inputs = setup_inputs


def setup_inputs(seed=0):
    import zlib

    import numpy as np

    out = dict(_drawn_inputs(seed))
    spreads = {}
    factors = {'ctx_2': 8.0,
     'c_ctx_2': 5.988,
     'b_mod_2': 8.0,
     'decay_w2_2': 8.0,
     'iclr_a0_2': 3.223,
     'iclr_a2_2': 2.901,
     'rwkv_k_k_2': 28.338,
     'rwkv_k_a_2': 8.0,
     'rwkv_gn_g_2': 8.0,
     'rwkv_gn_b_2': 64.0,
     'gqa_q_norm_2': 8.0,
     'gqa_k_norm_2': 8.0,
     'na_rpb_2': 64.0,
     'ln_b_2': 4.155}
    for name, (base, spread) in spreads.items():
        noise = np.random.default_rng([zlib.crc32(name.encode()), seed]).standard_normal(out[name].shape)
        drawn = base * np.exp(spread * noise) if base else spread * noise
        out[name] = __import__('jax').numpy.asarray(drawn.astype(out[name].dtype))
    for name, factor in factors.items():
        out[name] = (out[name] * factor).astype(out[name].dtype)
    return out
```

```python
import numpy as np
from contextlib import ExitStack

import concourse.bass as bass
from concourse import mybir

F32 = mybir.dt.float32
ALU = mybir.AluOpType
ACT = mybir.ActivationFunctionType
AX_X = mybir.AxisListType.X
ds = bass.ds

P = 128
TOP = 53208
D = 1024
KT = D // P
SEQ = 1024
CTX = 256
TOK2 = CTX + SEQ
EPS = 1e-6
LN_EPS = 1e-5
GN_EPS = 64e-5
FF = 2816
FFT = FF // P
NEG = -1e30
ALPHA = (2 * 2) ** 0.25
DECAY_MAX = float(np.exp(-0.5))
CREDIT = 64

GH, GN = 4, SEQ // P
LEVELS = 7
BH = 8
BUCKETS, MAX_DISTANCE = 32, 2048
GELEN = SEQ + P

CONST = {}
_at = 0
for _name, _n in [("ident", P), ("ones", P), ("block_ones", P), ("upper", P), ("lower", P), ("strict_low", P),
                  ("strict_up", P), ("swap", P), ("rope", P), ("lev", LEVELS * P), ("levT", LEVELS * P)]:
    CONST[_name] = (_at, _n)
    _at += _n
NCONST = _at


def constants():
    i = np.arange(P)
    c = np.zeros((P, NCONST), np.float32)

    def put(name, a):
        c[:, CONST[name][0]:CONST[name][0] + CONST[name][1]] = a

    put("ident", np.eye(P))
    put("ones", 1.0)
    put("block_ones", (i[:, None] // 64) == (i[None, :] // 64))
    put("upper", i[:, None] <= i[None, :])
    put("lower", i[:, None] >= i[None, :])
    put("strict_low", i[:, None] > i[None, :])
    put("strict_up", i[:, None] < i[None, :])
    put("swap", i[:, None] == (i[None, :] + 64) % P)
    rope = np.zeros((P, P), np.float32)
    for m in range(P):
        q, r = divmod(m % 32, 16)
        rope[m + 16 if q == 0 else m - 16, m] = -1.0 if q == 0 else 1.0
    put("rope", rope)
    lev = []
    for n in range(LEVELS):
        s = 1 << n
        same = (i[:, None] // (2 * s)) == (i[None, :] // (2 * s))
        lev.append(same & (i[:, None] // s % 2 == 1) & (i[None, :] // s % 2 == 0))
    put("lev", np.concatenate(lev, 1))
    put("levT", np.concatenate([m.T for m in lev], 1))
    return c


def dilated_table():
    dist = SEQ - 1 - np.arange(GELEN)
    d = np.maximum(dist, 1).astype(np.float32)
    half = BUCKETS // 2
    log_b = half + (np.log(d / half) / np.log(MAX_DISTANCE / half).astype(np.float32) * (BUCKETS - half)).astype(np.int32)
    b = np.where(dist < half, dist, np.minimum(log_b, BUCKETS - 1))
    count = np.zeros(GELEN)
    for window, dilation in ((128, 1), (512, 4), (2048, 16)):
        count += (dist >= 0) & (dist <= window) & (dist % dilation == 0)
    out = np.zeros((BUCKETS + 1, GELEN), np.float32)
    out[:BUCKETS] = (np.arange(BUCKETS)[:, None] == b[None]) & (dist >= 0)
    out[BUCKETS] = np.where(count > 0, np.log(np.maximum(count, 1)), NEG)
    return out


class Signal:

    def __init__(self, nc, ctx, name, start=0):
        self.sem = ctx.enter_context(nc.semaphore(name))
        self.planned = start


class Steps:

    def __init__(self, signal, names, iterations, by=1):
        names = names.split() if isinstance(names, str) else names
        self.sem, self.base, self.by = signal.sem, signal.planned, by
        self.index = {name: i for i, name in enumerate(names)}
        assert len(self.index) == len(names)
        signal.planned += by * len(names) * iterations

    def at(self, it, name):
        return it * (self.by * len(self.index)) + (self.base + self.by * (self.index[name] + 1))


    def before(self, it, n):
        return it * (self.by * len(self.index)) + (self.base + self.by * n)


class Core:

    def __init__(self, nc, ctx, io):
        self.nc, self.io = nc, io
        self.arena = ctx.enter_context(nc.sbuf_tensor("arena", [P, TOP], F32))
        self.psum = ctx.enter_context(nc.psum_tensor("psum", [P, 8, 512], F32))
        self.pe = Signal(nc, ctx, "pe_step", CREDIT)
        self.act = Signal(nc, ctx, "act_step", CREDIT)
        self.dve = Signal(nc, ctx, "dve_step", CREDIT)
        self.pool = Signal(nc, ctx, "pool_step", CREDIT)
        self.stage_end = Signal(nc, ctx, "stage_end")
        self.w_in = [Signal(nc, ctx, f"weights_in{i}") for i in range(8)]
        self.unit_used = [0] * 8
        self.moved = [Signal(nc, ctx, f"moved{i}") for i in range(24)]
        self.stages = []
        self.W = self.arena[:, 0:8192]
        self.C = self.arena[:, 8192:8192 + NCONST]
        self.free0 = 8192 + NCONST

    def const(self, name, n=None):
        a, w = CONST[name]
        if n is not None:
            return self.C[:, a + n * P:a + (n + 1) * P]
        return self.C[:, a:a + w]

    def region(self, start, *shape):
        n = int(np.prod(shape))
        assert start >= self.free0 and start + n <= TOP, (start, n)
        a = self.arena[:, start:start + n]
        if len(shape) == 1:
            return a
        if len(shape) == 2:
            return a.rearrange("p (a b) -> p a b", a=shape[0])
        return a.rearrange("p (a b c) -> p a b c", a=shape[0], b=shape[1])


class Stage:

    def __init__(self, core):
        self.c = core
        core.stages.append(self)
        core.stage_end.planned += 4
        self.meet = core.stage_end.planned

    def sp(self, sp): pass
    def run_pe(self, pe): pass
    def run_act(self, act): pass
    def run_dve(self, dve): pass
    def run_pool(self, pool): pass

    def finish(self, eng):
        eng.drain().then_inc(self.c.stage_end.sem, 1)
        eng.wait_ge(self.c.stage_end.sem, self.meet)


class Gemm(Stage):

    def __init__(self, core, mats, pieces, segments, moving, splits, kind, unroll, out, stage=None):
        super().__init__(core)
        self.mats, self.pieces, self.moving, self.splits, self.kind = mats, pieces, moving, splits, kind
        self.U, self.out, self.stage = unroll, out, stage
        self.tok = splits[-1][1]
        self.units = unroll * len(pieces)
        self.groups = len(splits) * len(mats)
        assert self.units <= 8 and (self.groups * unroll) % 4 == 0
        self.nmm = sum(k1 - k0 for _, k0, k1 in pieces) // len(mats)
        self.loops = []
        for col, n, first in segments:
            for start, count in ((0, n - n % unroll), (n - n % unroll, n % unroll)):
                if count:
                    self.loops.append(self.plan(col + start * P, first + start, count))

    def plan(self, col, first, n):
        c, whole = self.c, max(n // self.U, 1)
        U = min(self.U, n)
        plan = {"col": col, "first": first, "iters": whole, "U": U,
                "w_in": [c.w_in[i].planned for i in range(8)],
                "before": max(c.unit_used[i] for i in range(U * len(self.pieces))),
                "moved": [c.moved[i].planned for i in range(8)]}
        G = U * self.groups
        plan["pe"] = Steps(c.pe, [f"bank{g}" for g in range(G)], whole)
        plan["act"] = Steps(c.act, [f"bank{g}" for g in range(0, G, 2)], whole)
        plan["dve"] = Steps(c.dve, [f"bank{g}" for g in range(1, G, 2)], whole)
        for i in range(U * len(self.pieces)):
            c.w_in[i].planned += 16 * whole
            u = i // len(self.pieces)
            c.unit_used[i] = plan["pe"].at(whole - 1, f"bank{(u + 1) * self.groups - 1}")
        if self.kind == "store":
            for u in range(U):
                c.moved[u].planned += 16 * whole
        return plan

    def unit(self, i, kn):
        return self.c.W[:, i * 1024:i * 1024 + kn * P].rearrange("p (k f) -> p k f", k=kn)

    def each(self, eng, body, ahead=None):
        for L in self.loops:
            if ahead:
                ahead(L)
            if L["iters"] == 1:
                body(L, 0)
            else:
                with eng.Fori(0, L["iters"]) as it:
                    body(L, it)

    def sp(self, sp):
        def body(L, it):
            for u in range(L["U"]):
                if L["iters"] > 1:
                    sp.wait_ge(L["pe"].sem, L["pe"].before(it, (u + 1 - L["U"]) * self.groups))
                for j, (m, k0, k1) in enumerate(self.pieces):
                    i = u * len(self.pieces) + j
                    col = it * (L["U"] * P) + (L["col"] + u * P)
                    sp.dma_start(self.unit(i, k1 - k0), self.mats[m][:, k0:k1, ds(col, P)]).then_inc(self.c.w_in[i].sem, 16)

        def loop(L):
            if L["before"]:
                sp.wait_ge(L["pe"].sem, L["before"])

        self.each(sp, body, loop)

    def run_pe(self, pe):
        def body(L, it):
            g = 0
            for u in range(L["U"]):
                for s, (n0, n1) in enumerate(self.splits):
                    for m in range(len(self.mats)):
                        bank = g % 4
                        steps = L["act"] if g % 2 == 0 else L["dve"]
                        pe.wait_ge(steps.sem, steps.before(it, g // 2 - 1))
                        todo = [(j, k) for j, (mm, k0, k1) in enumerate(self.pieces) if mm == m for k in range(k0, k1)]
                        for x, (j, k) in enumerate(todo):
                            i = u * len(self.pieces) + j
                            k0, k1 = self.pieces[j][1:]
                            if s == 0 and k == k0:
                                pe.wait_ge(self.c.w_in[i].sem, it * 16 + (L["w_in"][i] + 16))
                            ins = pe.matmul(self.c.psum[:, bank, 0:n1 - n0], self.unit(i, k1 - k0)[:, k - k0, :],
                                            self.moving(k, n0, n1), start=(x == 0), stop=(x == len(todo) - 1))
                        ins.then_inc(L["pe"].sem, 1)
                        g += 1
        self.each(pe, body)

    def tile_out(self, L, it, u, n0, n1):
        if self.kind == "store":
            return self.stage[:, u, n0:n1]
        at = it * (L["U"] * self.tok) + ((L["first"] + u) * self.tok + n0)
        return self.out[:, ds(at, n1 - n0)]

    def evacuate(self, eng, parity):
        def body(L, it):
            g = 0
            for u in range(L["U"]):
                for s, (n0, n1) in enumerate(self.splits):
                    for m in range(len(self.mats)):
                        if g % 2 == parity:
                            bank = self.c.psum[:, g % 4, 0:n1 - n0]
                            eng.wait_ge(L["pe"].sem, L["pe"].at(it, f"bank{g}"))
                            mine = L["act"] if parity == 0 else L["dve"]
                            if self.kind == "store":
                                eng.wait_ge(self.c.moved[u].sem, it * 16 + L["moved"][u])
                                dst = self.tile_out(L, it, u, n0, n1)
                                ins = eng.copy(dst, bank) if parity == 0 else eng.tensor_copy(dst, bank)
                            elif self.kind == "keep":
                                dst = self.tile_out(L, it, u, n0, n1)
                                ins = eng.copy(dst, bank) if parity == 0 else eng.tensor_copy(dst, bank)
                            elif parity == 0:
                                eng.wait_ge(L["dve"].sem, L["dve"].before(it, g // 2 - 1))
                                ins = eng.activation(self.stage[:, g // 2 % 2, 0:n1 - n0], bank, ACT.Silu)
                            else:
                                eng.wait_ge(L["act"].sem, L["act"].at(it, f"bank{g - 1}"))
                                ins = eng.tensor_tensor(self.tile_out(L, it, u, n0, n1),
                                                        self.stage[:, g // 2 % 2, 0:n1 - n0], bank, ALU.mult)
                            ins.then_inc(mine.sem, 1)
                        g += 1
        self.each(eng, body)

    def run_act(self, act):
        self.evacuate(act, 0)

    def run_dve(self, dve):
        self.evacuate(dve, 1)

    def run_pool(self, pool):
        if self.kind != "store":
            return

        def body(L, it):
            for u in range(L["U"]):
                last = (u + 1) * self.groups - 1
                for name in ("act", "dve"):
                    g = last if last % 2 == ("act", "dve").index(name) else last - 1
                    if g >= 0:
                        pool.wait_ge(L[name].sem, L[name].at(it, f"bank{g}"))
                row = it * (L["U"] * P) + (L["first"] + u) * P
                pool.dma_start(self.out[ds(row, P), 0:self.tok], self.stage[:, u, 0:self.tok]).then_inc(self.c.moved[u].sem, 16)
        self.each(pool, body)
        for u in range(self.U):
            pool.wait_ge(self.c.moved[u].sem, self.stored[u])

    def close(self):
        self.stored = [self.c.moved[u].planned for u in range(8)]
        return self


class LoadTokens(Stage):

    def __init__(self, core, src, n_tiles, dst, t0, rows):
        super().__init__(core)
        self.src, self.n, self.dst, self.t0, self.rows = src, n_tiles, dst, t0, rows
        self.it = n_tiles // 2
        self.in_base = [core.moved[i].planned for i in range(2)]
        for i in range(2):
            core.moved[i].planned += 16 * self.it
        self.s_pe = Steps(core.pe, "a0 a1 b0 b1", self.it)
        self.s_act = Steps(core.act, "a0 b0", self.it)
        self.s_dve = Steps(core.dve, "a1 b1", self.it)

    def run_pool(self, pool):
        with pool.Fori(0, self.it) as it:
            for i in range(2):
                pool.wait_ge(self.s_pe.sem, self.s_pe.before(it, 2 * i - 2))
                pool.dma_start(self.rows[:, i, :], self.src[ds(it * (2 * P) + i * P, P), :]).then_inc(self.c.moved[i].sem, 16)

    def run_pe(self, pe):
        with pe.Fori(0, self.it) as it:
            for i in range(2):
                pe.wait_ge(self.c.moved[i].sem, it * 16 + (self.in_base[i] + 16))
                for h in range(2):
                    s = (self.s_act, self.s_dve)[h]
                    pe.wait_ge(s.sem, s.before(it, i - 1))
                    for k in range(4):
                        ins = pe.transpose(self.c.psum[:, 2 * i + h, k * P:(k + 1) * P],
                                           self.rows[:, i, (4 * h + k) * P:(4 * h + k + 1) * P], self.c.const("ident"))
                    ins.then_inc(self.s_pe.sem, 1)

    def copy_out(self, eng, h, s):
        with eng.Fori(0, self.it) as it:
            for i in range(2):
                eng.wait_ge(self.s_pe.sem, self.s_pe.at(it, "ab"[i] + str(h)))
                dst = self.dst[:, 4 * h:4 * h + 4, ds(it * (2 * P) + (self.t0 + i * P), P)]
                src = self.c.psum[:, 2 * i + h, :].rearrange("p (k t) -> p k t", k=4)
                (eng.copy(dst, src) if h == 0 else eng.tensor_copy(dst, src)).then_inc(s.sem, 1)

    def run_act(self, act):
        self.copy_out(act, 0, self.s_act)

    def run_dve(self, dve):
        self.copy_out(dve, 1, self.s_dve)


class StoreTokens(Stage):

    def __init__(self, core, src, t0, n_tiles, dst, rows):
        super().__init__(core)
        self.src, self.t0, self.n, self.dst, self.rows = src, t0, n_tiles, dst, rows
        self.base = [core.moved[i].planned for i in range(2)]
        for i in range(2):
            core.moved[i].planned += 16 * (n_tiles // 2)
        self.end = [core.moved[i].planned for i in range(2)]
        self.s_pe = Steps(core.pe, [f"t{t}" for t in range(n_tiles)], 1)
        self.s_act = Steps(core.act, [f"t{t}" for t in range(n_tiles)], 1)
        self.s_dve = Steps(core.dve, [f"t{t}" for t in range(n_tiles)], 1)

    def run_pe(self, pe):
        for t in range(self.n):
            pe.wait_ge(self.s_act.sem, self.s_act.before(0, t - 1))
            pe.wait_ge(self.s_dve.sem, self.s_dve.before(0, t - 1))
            for k in range(8):
                ins = pe.transpose(self.c.psum[:, 2 * (t % 2) + k // 4, k % 4 * P:(k % 4 + 1) * P],
                                   self.src[:, k, self.t0 + t * P:self.t0 + (t + 1) * P], self.c.const("ident"))
            ins.then_inc(self.s_pe.sem, 1)

    def copy_out(self, eng, h, s):
        for t in range(self.n):
            eng.wait_ge(self.s_pe.sem, self.s_pe.at(0, f"t{t}"))
            eng.wait_ge(self.c.moved[t % 2].sem, self.base[t % 2] + 16 * (t // 2))
            dst, src = self.rows[:, t % 2, 512 * h:512 * h + 512], self.c.psum[:, 2 * (t % 2) + h, :]
            (eng.copy(dst, src) if h == 0 else eng.tensor_copy(dst, src)).then_inc(s.sem, 1)

    def run_act(self, act):
        self.copy_out(act, 0, self.s_act)

    def run_dve(self, dve):
        self.copy_out(dve, 1, self.s_dve)

    def run_pool(self, pool):
        for t in range(self.n):
            pool.wait_ge(self.s_act.sem, self.s_act.at(0, f"t{t}"))
            pool.wait_ge(self.s_dve.sem, self.s_dve.at(0, f"t{t}"))
            pool.dma_start(self.dst[t * P:(t + 1) * P, :], self.rows[:, t % 2, :]).then_inc(self.c.moved[t % 2].sem, 16)
        for i in range(2):
            pool.wait_ge(self.c.moved[i].sem, self.end[i])


class Norm(Stage):

    def __init__(self, core, src, dst, g, T, tmp, mode, eps, b=None, center=False):
        super().__init__(core)
        self.src, self.dst, self.g, self.b, self.T, self.tmp = src, dst, g, b, T, tmp
        self.mode, self.eps, self.center = mode, eps, center
        self.splits = [(a, min(a + 512, T)) for a in range(0, T, 512)]
        self.s_pe = Steps(core.pe, (["mean"] if center else []) + [f"sum{k}" for k in range(KT)], 1)
        self.s_act = Steps(core.act, (["mean"] if center else []) + [f"sq{k}" for k in range(KT)] + ["std"]
                           + ([f"out{k}" for k in range(KT)] if b is not None else []), 1)
        self.s_dve = Steps(core.dve, ([f"cen{k}" for k in range(KT)] if center else []) + ["inv"]
                           + [f"out{k}" for k in range(KT)], 1)

    def run_pe(self, pe):
        c = self.c
        if self.center:
            for k in range(KT):
                for s, (a, b) in enumerate(self.splits):
                    ins = pe.matmul(c.psum[:, 3 + s, 0:b - a], c.const("ones"), self.src[:, k, a:b],
                                    start=(k == 0), stop=(k == KT - 1))
            ins.then_inc(self.s_pe.sem, 1)
        for k in range(KT):
            pe.wait_ge(self.s_act.sem, self.s_act.at(0, f"sq{k}"))
            for s, (a, b) in enumerate(self.splits):
                ins = pe.matmul(c.psum[:, s, 0:b - a], c.const("ones"), self.tmp[:, k % 2, a:b],
                                start=(k == 0), stop=(k == KT - 1))
            ins.then_inc(self.s_pe.sem, 1)

    def run_act(self, act):
        c = self.c
        if self.center:
            act.wait_ge(self.s_pe.sem, self.s_pe.at(0, "mean"))
            for s, (a, b) in enumerate(self.splits):
                ins = act.activation(self.tmp[:, 2, a:b], c.psum[:, 3 + s, 0:b - a], ACT.Copy, scale=1.0 / D)
            ins.then_inc(self.s_act.sem, 1)
        for k in range(KT):
            if self.center:
                act.wait_ge(self.s_dve.sem, self.s_dve.at(0, f"cen{k}"))
            if k >= 2:
                act.wait_ge(self.s_pe.sem, self.s_pe.at(0, f"sum{k - 2}"))
            act.activation(self.tmp[:, k % 2, :], self.src[:, k, :], ACT.Square).then_inc(self.s_act.sem, 1)
        act.wait_ge(self.s_pe.sem, self.s_pe.at(0, f"sum{KT - 1}"))
        for s, (a, b) in enumerate(self.splits):
            ins = act.activation(self.tmp[:, 3, a:b], c.psum[:, s, 0:b - a], ACT.Sqrt, scale=1.0 / D, bias=self.eps)
        ins.then_inc(self.s_act.sem, 1)
        if self.b is not None:
            for k in range(KT):
                act.wait_ge(self.s_dve.sem, self.s_dve.at(0, f"out{k}"))
                act.activation(self.dst[:, k, :], self.dst[:, k, :], ACT.Identity, bias=self.b(k)).then_inc(self.s_act.sem, 1)

    def run_dve(self, dve):
        if self.center:
            dve.wait_ge(self.s_act.sem, self.s_act.at(0, "mean"))
            for k in range(KT):
                dve.tensor_tensor(self.src[:, k, :], self.src[:, k, :], self.tmp[:, 2, :], ALU.subtract).then_inc(self.s_dve.sem, 1)
        dve.wait_ge(self.s_act.sem, self.s_act.at(0, "std"))
        dve.reciprocal(self.tmp[:, 3, :], self.tmp[:, 3, :]).then_inc(self.s_dve.sem, 1)
        dve.wait_ge(self.s_dve.sem, self.s_dve.at(0, "inv"))
        for k in range(KT):
            if self.mode == "write":
                ins = dve.scalar_tensor_tensor(out=self.dst[:, k, :], in0=self.src[:, k, :], scalar=self.g(k),
                                               in1=self.tmp[:, 3, :], op0=ALU.mult, op1=ALU.mult)
            else:
                dve.scalar_tensor_tensor(out=self.src[:, k, :], in0=self.src[:, k, :], scalar=self.g(k),
                                         in1=self.tmp[:, 3, :], op0=ALU.mult, op1=ALU.mult)
                dve.drain()
                ins = dve.tensor_tensor(self.dst[:, k, :], self.dst[:, k, :], self.src[:, k, :], ALU.add)
            ins.then_inc(self.s_dve.sem, 1)


class GdnPrep(Stage):

    def __init__(self, core, proj, cw, outs, buf):
        super().__init__(core)
        self.proj, self.cw, self.outs = proj, cw, outs
        n = SEQ + 3
        self.raw = [buf[:, i * 1028:i * 1028 + n] for i in range(3)]
        self.cv = [buf[:, 3084 + i * SEQ:3084 + (i + 1) * SEQ] for i in range(3)]
        self.sq = [buf[:, 6156 + i * SEQ:6156 + (i + 1) * SEQ] for i in range(2)]
        self.base = [core.moved[i].planned for i in range(3)]
        for i in range(3):
            core.moved[i].planned += 16 * GH
        self.s_pool = Steps(core.pool, "pads", 1)
        self.s_pe = Steps(core.pe, "sum0 sum1", GH)
        self.s_act = Steps(core.act, "silu0 silu1 silu2 sq0 sq1 std0 std1", GH)
        self.s_dve = Steps(core.dve, "conv0 conv1 conv2 out0 out1", GH)

    def run_pool(self, pool):
        for i in range(3):
            ins = pool.memset(self.raw[i][:, 0:3], 0.0)
        ins.then_inc(self.s_pool.sem, 1)
        with pool.Fori(0, GH) as h:
            for i in range(3):
                pool.wait_ge(self.s_dve.sem, self.s_dve.before(h, i - 4))
                pool.dma_start(self.raw[i][:, 3:], self.proj[ds(h * P + i * GH * P, P), 0:SEQ]).then_inc(self.c.moved[i].sem, 16)

    def run_pe(self, pe):
        with pe.Fori(0, GH) as h:
            for i in range(2):
                pe.wait_ge(self.s_act.sem, self.s_act.at(h, f"sq{i}"))
                for s in range(2):
                    ins = pe.matmul(self.c.psum[:, 2 * i + s, :], self.c.const("ones"), self.sq[i][:, 512 * s:512 * s + 512],
                                    start=True, stop=True)
                ins.then_inc(self.s_pe.sem, 1)

    def run_act(self, act):
        with act.Fori(0, GH) as h:
            for i in range(3):
                act.wait_ge(self.s_dve.sem, self.s_dve.at(h, f"conv{i}"))
                dst = self.cv[i] if i < 2 else self.outs[2][:, ds(h * SEQ, SEQ)]
                act.activation(dst, self.cv[i], ACT.Silu).then_inc(self.s_act.sem, 1)
            for i in range(2):
                act.wait_ge(self.s_act.sem, self.s_act.at(h, f"silu{i}"))
                act.wait_ge(self.s_dve.sem, self.s_dve.before(h, 0))
                act.activation(self.sq[i], self.cv[i], ACT.Square).then_inc(self.s_act.sem, 1)
            for i in range(2):
                act.wait_ge(self.s_pe.sem, self.s_pe.at(h, f"sum{i}"))
                act.activation(self.sq[i], self.c.psum[:, 2 * i:2 * i + 2, :].rearrange("p a b -> p (a b)"), ACT.Sqrt,
                               bias=1e-6).then_inc(self.s_act.sem, 1)

    def run_dve(self, dve):
        dve.wait_ge(self.s_pool.sem, self.s_pool.at(0, "pads"))
        with dve.Fori(0, GH) as h:
            for i in range(3):
                dve.wait_ge(self.c.moved[i].sem, h * 16 + (self.base[i] + 16))
                dve.wait_ge(self.s_act.sem, self.s_act.before(h, 0))
                tap = lambda w: self.cw[:, ds(h * 4 + (i * 16 + w), 1)]
                dve.tensor_scalar(self.cv[i], self.raw[i][:, 0:SEQ], tap(0), None, ALU.mult)
                for w in range(1, 4):
                    dve.drain()
                    ins = dve.scalar_tensor_tensor(out=self.cv[i], in0=self.raw[i][:, w:w + SEQ], scalar=tap(w),
                                                   in1=self.cv[i], op0=ALU.mult, op1=ALU.add)
                ins.then_inc(self.s_dve.sem, 1)
            for i in range(2):
                dve.wait_ge(self.s_act.sem, self.s_act.at(h, f"std{i}"))
                dve.reciprocal(self.sq[i], self.sq[i])
                dve.drain()
                dve.scalar_tensor_tensor(out=self.outs[i][:, ds(h * SEQ, SEQ)], in0=self.cv[i],
                                         scalar=float(P) ** -0.5 if i == 0 else 1.0, in1=self.sq[i],
                                         op0=ALU.mult, op1=ALU.mult).then_inc(self.s_dve.sem, 1)


class GdnGates(Stage):

    def __init__(self, core, hT, w, par, beta, g, buf):
        super().__init__(core)
        self.hT, self.w, self.par, self.beta, self.g = hT, w, par, beta, g
        self.wb = buf[:, 0:64].rearrange("p (k c) -> p k c", k=KT)
        self.t = [buf[:, 64 + i * 32:96 + i * 32] for i in range(5)]
        core.moved[0].planned += 16
        self.loaded = core.moved[0].planned
        self.s_pe = Steps(core.pe, "proj", 1)
        self.s_act = Steps(core.act, "beta expa abs exp ln", 1)
        self.s_dve = Steps(core.dve, "biased pos g", 1)

    def run_pool(self, pool):
        pool.dma_start(self.wb, self.w).then_inc(self.c.moved[0].sem, 16)

    def run_pe(self, pe):
        pe.wait_ge(self.c.moved[0].sem, self.loaded)
        for n in range(GN):
            for k in range(KT):
                ins = pe.matmul(self.c.psum[:, 0, 8 * n:8 * n + 8], self.hT[:, k, n * P:(n + 1) * P], self.wb[:, k, :],
                                start=(k == 0), stop=(k == KT - 1))
        ins.then_inc(self.s_pe.sem, 1)

    def run_act(self, act):
        v4 = lambda a: a.rearrange("p (n h) -> p n h", h=GH)
        act.wait_ge(self.s_pe.sem, self.s_pe.at(0, "proj"))
        z = self.c.psum[:, 0, 0:64].rearrange("p (n c) -> p n c", c=8)
        act.wait_ge(self.s_dve.sem, self.s_dve.at(0, "biased"))
        act.activation(v4(self.beta), z[:, :, 0:4], ACT.Sigmoid).then_inc(self.s_act.sem, 1)
        act.activation(self.t[0][:, 0:4], self.par[:, 0:4], ACT.Exp).then_inc(self.s_act.sem, 1)
        act.wait_ge(self.s_dve.sem, self.s_dve.at(0, "biased"))
        act.activation(self.t[2], self.t[1], ACT.Abs).then_inc(self.s_act.sem, 1)
        act.wait_ge(self.s_act.sem, self.s_act.at(0, "abs"))
        act.activation(self.t[2], self.t[2], ACT.Exp, scale=-1.0).then_inc(self.s_act.sem, 1)
        act.wait_ge(self.s_act.sem, self.s_act.at(0, "exp"))
        act.activation(self.t[3], self.t[2], ACT.Ln, bias=1.0).then_inc(self.s_act.sem, 1)

    def run_dve(self, dve):
        v4 = lambda a: a.rearrange("p (n h) -> p n h", h=GH)
        dve.wait_ge(self.s_pe.sem, self.s_pe.at(0, "proj"))
        z = self.c.psum[:, 0, 0:64].rearrange("p (n c) -> p n c", c=8)
        dve.tensor_tensor(v4(self.t[1]), z[:, :, 4:8], self.par[:, 4:8].unsqueeze(1).broadcast_to([P, GN, GH]),
                          ALU.add).then_inc(self.s_dve.sem, 1)
        dve.wait_ge(self.s_dve.sem, self.s_dve.at(0, "biased"))
        dve.tensor_scalar(self.t[4], self.t[1], 0.0, None, ALU.max).then_inc(self.s_dve.sem, 1)
        dve.wait_ge(self.s_act.sem, self.s_act.at(0, "ln"))
        dve.drain()
        dve.tensor_tensor(self.t[3], self.t[3], self.t[4], ALU.add)
        dve.drain()
        dve.scalar_tensor_tensor(out=v4(self.g), in0=v4(self.t[3]), scalar=-1.0,
                                 in1=self.t[0][:, 0:4].unsqueeze(1).broadcast_to([P, GN, GH]),
                                 op0=ALU.mult, op1=ALU.mult).then_inc(self.s_dve.sem, 1)


def heads4(a):
    return a.rearrange("p (h t) -> p h t", h=4)


def over_heads(m):
    return m.unsqueeze(1).broadcast_to([P, 4, P])


class Gdn(Stage):

    def __init__(self, core, q, k, v, beta, g, out, buf):
        super().__init__(core)
        self.q, self.k, self.v, self.beta, self.g, self.out = q, k, v, beta, g, out
        names = ("kc qc vc gbc dd D Ds A AT X XT MT0 MT1 Y attn ktok vtok kbg kd vb wT vnew qd rowexp S").split()
        self.b = {n: buf[:, i * 512:(i + 1) * 512] for i, n in enumerate(names)}
        self.b["DT"] = self.b["dd"]
        at = len(names) * 512
        for n in ("gn", "bn", "gcol", "eg", "bg", "kdsc"):
            self.b[n] = buf[:, at:at + 4]
            at += 4
        self.s_pool = Steps(core.pool, ["kc", "qc", "vc", "g", "X0", "XT0"] + [f"mt{l}" for l in range(1, LEVELS)], GN)
        self.s_pe = Steps(core.pe, ["gates", "scores", "ktok", "vtok", "turn_A", "turn_D"]
                          + [f"{x}{l}" for l in range(1, LEVELS) for x in ("y", "x")] + ["w", "vnew", "o", "dS"], GN)
        self.s_act = Steps(core.act, ["rowexp", "eg", "exp", "kdsc", "AT", "DT"] + [f"y{l}" for l in range(1, LEVELS)]
                           + ["kbg", "kd", "vb", "w", "vnew", "o"], GN)
        self.s_dve = Steps(core.dve, ["S0", "dd", "D", "A", "bg", "kdsc", "attn", "qd"] + [f"x{l}" for l in range(1, LEVELS)] + ["S"], GN)

    def run_pool(self, pool):
        b, s, A, Dv, E = self.b, self.s_pool, self.s_act, self.s_dve, self.s_pe
        with pool.Fori(0, GN) as n:
            for x, src in (("kc", self.k), ("qc", self.q), ("vc", self.v)):
                pool.wait_ge(E.sem, E.before(n, 0))
                pool.wait_ge(Dv.sem, Dv.before(n, 0))
                pool.tensor_copy(heads4(b[x]), src.rearrange("p (h t) -> p h t", h=GH)[:, :, ds(n * P, P)]).then_inc(s.sem, 1)
            pool.wait_ge(A.sem, A.before(n, 0))
            pool.tensor_copy(b["gn"], self.g[:, ds(n * GH, GH)])
            pool.tensor_copy(b["bn"], self.beta[:, ds(n * GH, GH)])
            pool.drain()
            pool.tensor_copy(heads4(b["gbc"]), b["gn"].unsqueeze(2).broadcast_to([P, GH, P])).then_inc(s.sem, 1)
            pool.wait_ge(Dv.sem, Dv.at(n, "A"))
            pool.tensor_tensor(heads4(b["X"]), heads4(b["A"]), over_heads(self.c.const("lev", 0)), ALU.mult)
            pool.drain()
            pool.tensor_tensor(heads4(b["X"]), over_heads(self.c.const("ident")), heads4(b["X"]), ALU.subtract).then_inc(s.sem, 1)
            pool.wait_ge(A.sem, A.at(n, "AT"))
            pool.tensor_tensor(heads4(b["XT"]), heads4(b["AT"]), over_heads(self.c.const("levT", 0)), ALU.mult)
            pool.drain()
            pool.tensor_tensor(heads4(b["XT"]), over_heads(self.c.const("ident")), heads4(b["XT"]), ALU.subtract).then_inc(s.sem, 1)
            for l in range(1, LEVELS):
                if l > 2:
                    pool.wait_ge(E.sem, E.at(n, f"y{l - 2}"))
                pool.tensor_tensor(heads4(b[f"MT{l % 2}"]), heads4(b["AT"]), over_heads(self.c.const("levT", l)),
                                   ALU.mult).then_inc(s.sem, 1)

    def run_pe(self, pe):
        b, s, A, Dv, O = self.b, self.s_pe, self.s_act, self.s_dve, self.s_pool
        ps = self.c.psum
        hh = lambda name, h: b[name][:, h * P:(h + 1) * P]

        def four(bank, lhs, rhs, more=None):
            for h in range(GH):
                ins = pe.matmul(ps[:, bank, h * P:(h + 1) * P], lhs(h), rhs(h), start=True, stop=(more is None))
                if more is not None:
                    ins = pe.matmul(ps[:, bank, h * P:(h + 1) * P], more[0](h), more[1](h), start=False, stop=True)
            return ins

        def turn(bank, name):
            for h in range(GH):
                ins = pe.transpose(ps[:, bank, h * P:(h + 1) * P], hh(name, h), self.c.const("ident"))
            return ins

        up = self.c.const("upper")
        with pe.Fori(0, GN) as n:
            pe.wait_ge(O.sem, O.at(n, "g"))
            pe.wait_ge(A.sem, A.before(n, 0))
            pe.wait_ge(Dv.sem, Dv.before(n, 0))
            pe.matmul(ps[:, 0, 0:GH], up, b["gn"], start=True, stop=True)
            four(1, lambda h: hh("gbc", h), lambda h: up).then_inc(s.sem, 1)
            four(2, lambda h: hh("kc", h), lambda h: hh("kc", h))
            four(3, lambda h: hh("kc", h), lambda h: hh("qc", h)).then_inc(s.sem, 1)
            turn(4, "kc").then_inc(s.sem, 1)
            turn(5, "vc").then_inc(s.sem, 1)
            pe.wait_ge(Dv.sem, Dv.at(n, "A"))
            turn(6, "A").then_inc(s.sem, 1)
            turn(7, "D").then_inc(s.sem, 1)
            for l in range(1, LEVELS):
                pe.wait_ge(O.sem, O.at(n, f"mt{l}"))
                if l > 1:
                    pe.wait_ge(Dv.sem, Dv.at(n, f"x{l - 1}"))
                if l == 1:
                    pe.wait_ge(Dv.sem, Dv.at(n, "attn"))
                four(0, lambda h: hh(f"MT{l % 2}", h), lambda h: hh("X", h)).then_inc(s.sem, 1)
                pe.wait_ge(A.sem, A.at(n, f"y{l}"))
                if l < LEVELS - 1:
                    four(1, lambda h: hh("XT", h), lambda h: hh("Y", h))
                four(2, lambda h: hh("Y", h), lambda h: hh("XT", h)).then_inc(s.sem, 1)
            pe.wait_ge(Dv.sem, Dv.at(n, f"x{LEVELS - 1}"))
            pe.wait_ge(A.sem, A.at(n, "kbg"))
            four(3, lambda h: hh("kbg", h), lambda h: hh("XT", h)).then_inc(s.sem, 1)
            pe.wait_ge(A.sem, A.at(n, "w"))
            pe.wait_ge(Dv.sem, Dv.at(n, "S0"))
            four(6, lambda h: hh("XT", h), lambda h: hh("vb", h),
                 (lambda h: hh("wT", h), lambda h: hh("S", h))).then_inc(s.sem, 1)
            pe.wait_ge(Dv.sem, Dv.at(n, "qd"))
            pe.wait_ge(A.sem, A.at(n, "vnew"))
            four(7, lambda h: hh("S", h), lambda h: hh("qd", h),
                 (lambda h: hh("vnew", h), lambda h: hh("attn", h))).then_inc(s.sem, 1)
            four(0, lambda h: hh("kd", h), lambda h: hh("vnew", h)).then_inc(s.sem, 1)

    def run_act(self, act):
        b, s, E, Dv, O = self.b, self.s_act, self.s_pe, self.s_dve, self.s_pool
        ps = self.c.psum
        with act.Fori(0, GN) as n:
            act.wait_ge(Dv.sem, Dv.at(n, "dd"))
            act.activation(b["rowexp"], ps[:, 1, :], ACT.Exp).then_inc(s.sem, 1)
            act.activation(b["eg"], ps[:, 0, 0:GH], ACT.Exp).then_inc(s.sem, 1)
            act.wait_ge(Dv.sem, Dv.at(n, "dd"))
            act.activation(b["D"], b["dd"], ACT.Exp, scale=-1.0).then_inc(s.sem, 1)
            act.wait_ge(Dv.sem, Dv.at(n, "kdsc"))
            act.activation(b["kdsc"], b["kdsc"], ACT.Exp).then_inc(s.sem, 1)
            act.wait_ge(E.sem, E.at(n, "turn_A"))
            act.copy(b["AT"], ps[:, 6, :]).then_inc(s.sem, 1)
            act.wait_ge(E.sem, E.at(n, "turn_D"))
            act.copy(b["DT"], ps[:, 7, :]).then_inc(s.sem, 1)
            for l in range(1, LEVELS):
                act.wait_ge(E.sem, E.at(n, f"y{l}"))
                act.copy(b["Y"], ps[:, 0, :]).then_inc(s.sem, 1)
            act.wait_ge(s.sem, s.at(n, "kdsc"))
            for name, bank, by in (("kbg", 4, "bg"), ("kd", 4, "kdsc"), ("vb", 5, "bn")):
                for h in range(GH):
                    ins = act.activation(b[name][:, h * P:(h + 1) * P], ps[:, bank, h * P:(h + 1) * P], ACT.Copy,
                                         scale=b[by][:, h:h + 1])
                ins.then_inc(s.sem, 1)
            act.wait_ge(E.sem, E.at(n, "w"))
            act.activation(b["wT"], ps[:, 3, :], ACT.Copy, scale=-1.0).then_inc(s.sem, 1)
            act.wait_ge(E.sem, E.at(n, "vnew"))
            act.copy(b["vnew"], ps[:, 6, :]).then_inc(s.sem, 1)
            act.wait_ge(E.sem, E.at(n, "o"))
            act.copy(self.out[:, 0:GH, ds(n * P, P)], heads4(ps[:, 7, :])).then_inc(s.sem, 1)

    def run_dve(self, dve):
        b, s, E, A, O = self.b, self.s_dve, self.s_pe, self.s_act, self.s_pool
        ps = self.c.psum
        dve.memset(b["S"], 0.0)
        with dve.Fori(0, GN) as n:
            dve.wait_ge(E.sem, E.at(n, "gates"))
            dve.tensor_copy(b["gcol"], ps[:, 0, 0:GH])
            dve.drain().then_inc(s.sem, 1)
            for h in range(GH):
                ins = dve.tensor_scalar(b["dd"][:, h * P:(h + 1) * P], ps[:, 1, h * P:(h + 1) * P], b["gcol"][:, h:h + 1],
                                        0.0, ALU.subtract, ALU.max)
            ins.then_inc(s.sem, 1)
            dve.wait_ge(A.sem, A.at(n, "exp"))
            dve.tensor_tensor(heads4(b["D"]), heads4(b["D"]), over_heads(self.c.const("lower")), ALU.mult)
            dve.drain().then_inc(s.sem, 1)
            dve.tensor_tensor(heads4(b["Ds"]), heads4(b["D"]), over_heads(self.c.const("strict_low")), ALU.mult)
            dve.drain()
            dve.wait_ge(E.sem, E.at(n, "scores"))
            for h in range(GH):
                ins = dve.scalar_tensor_tensor(out=b["A"][:, h * P:(h + 1) * P], in0=ps[:, 2, h * P:(h + 1) * P],
                                               scalar=b["bn"][:, h:h + 1], in1=b["Ds"][:, h * P:(h + 1) * P],
                                               op0=ALU.mult, op1=ALU.mult)
            ins.then_inc(s.sem, 1)
            dve.tensor_tensor(b["bg"], b["bn"], b["eg"], ALU.mult).then_inc(s.sem, 1)
            dve.tensor_tensor(b["kdsc"], heads4(ps[:, 1, :])[:, :, P - 1], b["gcol"], ALU.subtract).then_inc(s.sem, 1)
            dve.wait_ge(A.sem, A.at(n, "DT"))
            dve.tensor_tensor(b["attn"], ps[:, 3, :], b["DT"], ALU.mult).then_inc(s.sem, 1)
            dve.wait_ge(O.sem, O.at(n, "qc"))
            dve.tensor_tensor(b["qd"], b["qc"], b["rowexp"], ALU.mult).then_inc(s.sem, 1)
            for l in range(1, LEVELS):
                dve.wait_ge(E.sem, E.at(n, f"x{l}"))
                if l < LEVELS - 1:
                    dve.tensor_tensor(b["X"], b["X"], ps[:, 1, :], ALU.subtract)
                dve.tensor_tensor(b["XT"], b["XT"], ps[:, 2, :], ALU.subtract).then_inc(s.sem, 1)
            dve.wait_ge(E.sem, E.at(n, "dS"))
            for h in range(GH):
                ins = dve.scalar_tensor_tensor(out=b["S"][:, h * P:(h + 1) * P], in0=b["S"][:, h * P:(h + 1) * P],
                                               scalar=b["rowexp"][:, (h + 1) * P - 1:(h + 1) * P],
                                               in1=ps[:, 0, h * P:(h + 1) * P], op0=ALU.mult, op1=ALU.add)
            ins.then_inc(s.sem, 1)


class GdnOut(Stage):

    def __init__(self, core, mix, gate_rows, onorm, buf):
        super().__init__(core)
        self.mix, self.gate_rows, self.onorm = mix, gate_rows, onorm
        self.gate = [buf[:, i * SEQ:(i + 1) * SEQ] for i in range(2)]
        self.sq = [buf[:, (2 + i) * SEQ:(3 + i) * SEQ] for i in range(2)]
        self.base = [core.moved[i].planned for i in range(2)]
        for i in range(2):
            core.moved[i].planned += 16 * (GH // 2)
        self.s_pe = Steps(core.pe, "sum0 sum1", GH // 2)
        self.s_act = Steps(core.act, "sq0 sq1 std0 std1 gate0 gate1", GH // 2)
        self.s_dve = Steps(core.dve, "out0 out1", GH // 2)

    def run_pool(self, pool):
        for it in range(GH // 2):
            for i in range(2):
                pool.wait_ge(self.s_dve.sem, self.s_dve.before(it, 0))
                pool.dma_start(self.gate[i], self.gate_rows[ds((2 * it + i) * P, P), 0:SEQ]).then_inc(self.c.moved[i].sem, 16)

    def run_pe(self, pe):
        for it in range(GH // 2):
            for i in range(2):
                pe.wait_ge(self.s_act.sem, self.s_act.at(it, f"sq{i}"))
                for s in range(2):
                    ins = pe.matmul(self.c.psum[:, 2 * i + s, :], self.c.const("ones"), self.sq[i][:, 512 * s:512 * s + 512],
                                    start=True, stop=True)
                ins.then_inc(self.s_pe.sem, 1)

    def run_act(self, act):
        for it in range(GH // 2):
            for i in range(2):
                act.wait_ge(self.s_dve.sem, self.s_dve.before(it, 0))
                act.activation(self.sq[i], self.mix[:, 2 * it + i, :], ACT.Square).then_inc(self.s_act.sem, 1)
            for i in range(2):
                act.wait_ge(self.s_pe.sem, self.s_pe.at(it, f"sum{i}"))
                act.activation(self.sq[i], self.c.psum[:, 2 * i:2 * i + 2, :].rearrange("p a b -> p (a b)"), ACT.Sqrt,
                               scale=1.0 / P, bias=EPS).then_inc(self.s_act.sem, 1)
            for i in range(2):
                act.wait_ge(self.c.moved[i].sem, it * 16 + self.base[i] + 16)
                act.activation(self.gate[i], self.gate[i], ACT.Silu).then_inc(self.s_act.sem, 1)

    def run_dve(self, dve):
        for it in range(GH // 2):
            for i in range(2):
                m = self.mix[:, 2 * it + i, :]
                dve.wait_ge(self.s_act.sem, self.s_act.at(it, f"gate{i}"))
                dve.reciprocal(self.sq[i], self.sq[i])
                dve.drain()
                dve.scalar_tensor_tensor(out=m, in0=m, scalar=self.onorm, in1=self.sq[i], op0=ALU.mult, op1=ALU.mult)
                dve.drain()
                dve.tensor_tensor(m, m, self.gate[i], ALU.mult).then_inc(self.s_dve.sem, 1)


class Attention(Stage):

    def __init__(self, core, pairs, n_q, n_k, units, bias, loads, out, at, pt_banks, pool_bias=None, once=None):
        super().__init__(core)
        R = core.region
        self.pairs, self.n_q, self.n_k, self.units, self.bias, self.loads, self.out = pairs, n_q, n_k, units, bias, loads, out
        self.pool_bias, self.once = pool_bias, once
        self.nkt = n_k // P
        self.width = max(sum(n for _, n in segs) for _, segs in units)
        self.lb = -(-self.width // 512)
        self.ptb = pt_banks
        self.ob = [b for b in range(2 * self.lb, 8) if b not in pt_banks]
        assert self.ob
        self.q = R(at, n_q); at += n_q
        self.k = R(at, n_k); at += n_k
        self.v = R(at, n_k); at += n_k
        self.v1 = R(at, self.nkt, 2, P); at += self.nkt * 2 * P
        self.p = R(at, 2, self.width); at += 2 * self.width
        self.pt = R(at, 2, self.width // P, P); at += 2 * self.width
        self.m = R(at, 2); at += 2
        self.rec = R(at, 512); at += 512
        if pool_bias:
            self.pb = R(at, 2, self.width); at += 2 * self.width
        self.end = at
        n = len(units)
        self.all = [(j, t) for j in range(2) for t in range(n)]
        self.outs = []
        for j in range(2):
            for a in range(0, n, 4):
                b = min(a + 4, n)
                self.outs.append((j * n + b - 1, j * n + a, b - a))
        self.ngroups = lambda u: -(-self.widths(u) // 512)
        self.nload = len(loads(0, self))
        self.base = core.moved[0].planned
        core.moved[0].planned += 16 * self.nload * pairs
        self.once_base = core.moved[1].planned
        if once:
            core.moved[1].planned += 16 * len(once)
        vb = -(-self.nkt // 4)
        U = range(len(self.all))
        self.s_pe = Steps(core.pe, [f"v{b}" for b in range(vb)] + ["qk0"] + [x for u in U for x in (
            ([f"qk{u + 1}"] if u + 1 < len(self.all) else []) + [f"t{u}_{g}" for g in range(self.ngroups(u))] + [f"pv{u}"])], pairs)
        self.s_act = Steps(core.act, ["e0"] + [x for u in U for x in (
            [f"pt{u}_{g}" for g in range(self.ngroups(u))] + ([f"e{u + 1}"] if u + 1 < len(self.all) else []))], pairs)
        self.s_dve = Steps(core.dve, ["q"] + [f"v{b}" for b in range(vb)] + ["m0"] + [x for u in U for x in (
            ([f"m{u + 1}"] if u + 1 < len(self.all) else []) + [f"out{u}" for o in self.outs if o[0] == u])], pairs)
        self.s_ones = Steps(core.pool, "ones", 1)
        self.s_pool = Steps(core.pool, [f"bias{u}" for u in U], pairs) if pool_bias else None

    def widths(self, u):
        return sum(n for _, n in self.units[self.all[u][1]][1])

    def run_pool(self, pool):
        for x, (dst, src) in enumerate(self.once or []):
            pool.dma_start(dst, src).then_inc(self.c.moved[1].sem, 16)
        if self.pool_bias:
            pool.memset(self.pb[:, :, :], 0.0)
        pool.memset(self.v1[:, :, :, :], 1.0)
        pool.drain().then_inc(self.s_ones.sem, 1)
        if self.once:
            pool.wait_ge(self.c.moved[1].sem, self.once_base + 16 * len(self.once))
        with pool.Fori(0, self.pairs) as it:
            pool.wait_ge(self.s_pe.sem, self.s_pe.before(it, 0))
            pool.wait_ge(self.s_dve.sem, self.s_dve.before(it, 0))
            for dst, src in self.loads(it, self):
                pool.dma_start(dst, src).then_inc(self.c.moved[0].sem, 16)
            if self.pool_bias:
                pool.wait_ge(self.c.moved[0].sem, (it + 1) * (16 * self.nload) + self.base)
                for u, (j, t) in enumerate(self.all):
                    if u >= 2:
                        pool.wait_ge(self.s_dve.sem, self.s_dve.at(it, f"m{u - 2}"))
                    self.pool_bias(pool, j, t, self.pb[:, u % 2, :]).then_inc(self.s_pool.sem, 1)

    def run_pe(self, pe):
        ps, E, A, Dv = self.c.psum, self.s_pe, self.s_act, self.s_dve
        ident = self.c.const("ident")
        with pe.Fori(0, self.pairs) as it:
            pe.wait_ge(self.c.moved[0].sem, (it + 1) * (16 * self.nload) + self.base)
            pe.wait_ge(A.sem, A.before(it, 0))
            pe.wait_ge(Dv.sem, Dv.before(it, 0))
            for b in range(-(-self.nkt // 4)):
                for kt in range(4 * b, min(4 * b + 4, self.nkt)):
                    ins = pe.transpose(ps[:, b, kt % 4 * P:(kt % 4 + 1) * P], self.v[:, kt * P:(kt + 1) * P], ident)
                ins.then_inc(E.sem, 1)

            def qk(u):
                j, t = self.all[u]
                q, segs = self.units[t]
                if u == 0:
                    pe.wait_ge(Dv.sem, Dv.at(it, f"v{-(-self.nkt // 4) - 1}"))
                elif u >= 2 and self.bias:
                    pe.wait_ge(Dv.sem, Dv.at(it, f"m{u - 2}"))
                elif u >= 2:
                    pe.wait_ge(A.sem, A.at(it, f"e{u - 2}"))
                rows = slice(64 * j, 64 * j + 64)
                at = 0
                for k0, n in segs:
                    while n:
                        m = min(n, 512 - at % 512)
                        ins = pe.matmul(ps[:, u % 2 * self.lb + at // 512, at % 512:at % 512 + m],
                                        self.q[rows, q * P:(q + 1) * P], self.k[rows, k0:k0 + m], start=True, stop=True)
                        at, k0, n = at + m, k0 + m, n - m
                ins.then_inc(E.sem, 1)

            turned = []
            qk(0)
            for u, (j, t) in enumerate(self.all):
                if u + 1 < len(self.all):
                    qk(u + 1)
                w = self.widths(u)
                for g in range(self.ngroups(u)):
                    if g == 0:
                        pe.wait_ge(A.sem, A.at(it, f"e{u}"))
                    if len(turned) >= len(self.ptb):
                        pe.wait_ge(A.sem, A.at(it, "pt" + turned[-len(self.ptb)]))
                    bank = self.ptb[len(turned) % len(self.ptb)]
                    for c in range(4 * g, min(4 * g + 4, w // P)):
                        ins = pe.transpose(ps[:, bank, c % 4 * P:(c % 4 + 1) * P], self.p[:, u % 2, c * P:(c + 1) * P], ident)
                    ins.then_inc(E.sem, 1)
                    turned.append(f"{u}_{g}")
                o = [x for x in range(len(self.outs)) if self.outs[x][1] <= u <= self.outs[x][0]][0]
                if u == self.outs[o][1] and o >= len(self.ob):
                    pe.wait_ge(Dv.sem, Dv.at(it, f"out{self.outs[o - len(self.ob)][0]}"))
                pe.wait_ge(A.sem, A.at(it, f"pt{u}_{self.ngroups(u) - 1}"))
                s = u - self.outs[o][1]
                tiles = [k0 // P + x for k0, n in self.units[t][1] for x in range(n // P)]
                for c, kt in enumerate(tiles):
                    ins = pe.matmul(ps[:, self.ob[o % len(self.ob)], s * P:(s + 1) * P], self.v1[:, kt, j, :],
                                    self.pt[:, u % 2, c, :], start=(c == 0), stop=(c == len(tiles) - 1))
                ins.then_inc(E.sem, 1)

    def run_act(self, act):
        ps, E, A, Dv = self.c.psum, self.s_pe, self.s_act, self.s_dve
        with act.Fori(0, self.pairs) as it:
            def ex(u):
                w = self.widths(u)
                act.wait_ge(Dv.sem, Dv.at(it, f"m{u}"))
                if u >= 2:
                    act.wait_ge(E.sem, E.at(it, f"t{u - 2}_{self.ngroups(u - 2) - 1}"))
                if self.bias:
                    ins = act.activation(self.p[:, u % 2, 0:w], self.p[:, u % 2, 0:w], ACT.Exp, bias=self.m[:, u % 2:u % 2 + 1])
                else:
                    src = ps[:, u % 2 * self.lb:(u % 2 + 1) * self.lb, :].rearrange("p a b -> p (a b)")[:, 0:w]
                    ins = act.activation(self.p[:, u % 2, 0:w], src, ACT.Exp, bias=self.m[:, u % 2:u % 2 + 1])
                ins.then_inc(A.sem, 1)

            ex(0)
            turned = 0
            for u in range(len(self.all)):
                w = self.widths(u)
                for g in range(self.ngroups(u)):
                    act.wait_ge(E.sem, E.at(it, f"t{u}_{g}"))
                    if g == 0 and u >= 2:
                        act.wait_ge(E.sem, E.at(it, f"pv{u - 2}"))
                    n = min(512, w - 512 * g)
                    act.copy(self.pt[:, u % 2, 4 * g:4 * g + n // P, :].rearrange("p a b -> p (a b)"),
                             ps[:, self.ptb[turned % len(self.ptb)], 0:n]).then_inc(A.sem, 1)
                    turned += 1
                if u + 1 < len(self.all):
                    ex(u + 1)

    def run_dve(self, dve):
        ps, E, A, Dv = self.c.psum, self.s_pe, self.s_act, self.s_dve
        dve.wait_ge(self.s_ones.sem, self.s_ones.at(0, "ones"))
        with dve.Fori(0, self.pairs) as it:
            dve.wait_ge(self.c.moved[0].sem, (it + 1) * (16 * self.nload) + self.base)
            dve.tensor_scalar(self.q, self.q, 0.125, None, ALU.mult).then_inc(Dv.sem, 1)
            for b in range(-(-self.nkt // 4)):
                dve.wait_ge(E.sem, E.at(it, f"v{b}"))
                n = min(4, self.nkt - 4 * b)
                src = ps[:, b, 0:n * P].rearrange("p (k f) -> p k f", k=n)
                for j in range(2):
                    ins = dve.tensor_copy(self.v1[:, 4 * b:4 * b + n, j, 64 * j:64 * j + 64], src[:, :, 64 * j:64 * j + 64])
                ins.then_inc(Dv.sem, 1)

            def mx(u):
                j, t = self.all[u]
                w = self.widths(u)
                dve.wait_ge(E.sem, E.at(it, f"qk{u}"))
                src = ps[:, u % 2 * self.lb:(u % 2 + 1) * self.lb, :].rearrange("p a b -> p (a b)")[:, 0:w]
                if u >= 2:
                    dve.wait_ge(A.sem, A.at(it, f"e{u - 2}"))
                if self.bias:
                    if self.pool_bias:
                        dve.wait_ge(self.s_pool.sem, self.s_pool.at(it, f"bias{u}"))
                    if u >= 2:
                        dve.wait_ge(E.sem, E.at(it, f"t{u - 2}_{self.ngroups(u - 2) - 1}"))
                    elif u == 0:
                        dve.wait_ge(self.c.moved[0].sem, (it + 1) * (16 * self.nload) + self.base)
                    dve.tensor_tensor(self.p[:, u % 2, 0:w], src, self.bias(self, u, j, t), ALU.add)
                    dve.drain()
                    src = self.p[:, u % 2, 0:w]
                dve.tensor_reduce(self.m[:, u % 2:u % 2 + 1], src, AX_X, ALU.max, negate=True).then_inc(Dv.sem, 1)

            mx(0)
            for u in range(len(self.all)):
                if u + 1 < len(self.all):
                    mx(u + 1)
                for o, (last, first, n) in enumerate(self.outs):
                    if last == u:
                        j = self.all[u][0]
                        dve.wait_ge(E.sem, E.at(it, f"pv{u}"))
                        bank = ps[:, self.ob[o % len(self.ob)], 0:n * P]
                        rows, sums = slice(64 * j, 64 * j + 64), slice(64 - 64 * j, 128 - 64 * j)
                        dve.reciprocal(self.rec[rows, 0:n * P], bank[sums, :])
                        dve.drain()
                        q0 = self.units[self.all[first][1]][0] * P
                        dve.tensor_tensor(self.out(it, rows, q0, n * P), bank[rows, :], self.rec[rows, 0:n * P],
                                          ALU.mult).then_inc(Dv.sem, 1)


class DilatedBias(Stage):

    def __init__(self, core, rel, table, flat, band, buf):
        super().__init__(core)
        self.rel, self.table, self.flat, self.band = rel, table, flat, band
        self.r = buf[0:BUCKETS + 1, 0:BH]
        self.t = buf[0:BUCKETS + 1, 8:8 + GELEN]
        self.f = buf[0:BH, 8 + GELEN:8 + 2 * GELEN]
        self.base = core.moved[0].planned
        core.moved[0].planned += 16 * 4
        self.s_pe = Steps(core.pe, "f", 1)
        self.s_act = Steps(core.act, "f", 1)

    def run_pool(self, pool):
        pool.dma_start(self.r, self.rel).then_inc(self.c.moved[0].sem, 16)
        pool.dma_start(self.t, self.table).then_inc(self.c.moved[0].sem, 16)
        pool.wait_ge(self.s_act.sem, self.s_act.at(0, "f"))
        pool.dma_start(self.flat, self.f).then_inc(self.c.moved[0].sem, 16)
        pool.wait_ge(self.c.moved[0].sem, self.base + 48)
        for_all = self.flat.unsqueeze(1).broadcast_to([BH, P, GELEN])
        pool.dma_start(self.band, for_all).then_inc(self.c.moved[0].sem, 16)
        pool.wait_ge(self.c.moved[0].sem, self.base + 64)

    def run_pe(self, pe):
        pe.wait_ge(self.c.moved[0].sem, self.base + 32)
        for s in range(3):
            n = min(512, GELEN - 512 * s)
            ins = pe.matmul(self.c.psum[0:BH, s, 0:n], self.r, self.t[:, 512 * s:512 * s + n], start=True, stop=True)
        ins.then_inc(self.s_pe.sem, 1)

    def run_act(self, act):
        act.wait_ge(self.s_pe.sem, self.s_pe.at(0, "f"))
        for s in range(3):
            n = min(512, GELEN - 512 * s)
            ins = act.copy(self.f[:, 512 * s:512 * s + n], self.c.psum[0:BH, s, 0:n])
        ins.then_inc(self.s_act.sem, 1)


class LoadInputs(Stage):

    def __init__(self, core, pairs):
        super().__init__(core)
        self.pairs = pairs
        core.moved[0].planned += 16 * len(pairs)
        self.loaded = core.moved[0].planned

    def run_pool(self, pool):
        for dst, src in self.pairs:
            pool.dma_start(dst, src).then_inc(self.c.moved[0].sem, 16)
        pool.wait_ge(self.c.moved[0].sem, self.loaded)


PAR1 = {"g_mix_pre": 8, "g_mix_post": 8, "g_ffn_pre": 8, "g_ffn_post": 8, "conv_w": 48, "onorm_g": 1, "gates": 8}
PARAM = {}
_at = 0
for _name, _n in PAR1.items():
    PARAM[_name] = (_at, _n)
    _at += _n
NPAR = _at


class CopyTiles(Stage):

    def __init__(self, core, dst, src):
        super().__init__(core)
        self.dst, self.src = dst, src

    def run_act(self, act):
        for k in range(0, KT, 2):
            act.copy(self.dst[:, k, :], self.src[:, k, :])

    def run_dve(self, dve):
        for k in range(1, KT, 2):
            dve.tensor_copy(self.dst[:, k, :], self.src[:, k, :])


class CondVector(Stage):

    def __init__(self, core, cond, out):
        super().__init__(core)
        self.cond, self.out = cond, out

    def run_act(self, act):
        act.activation(self.out, self.cond, ACT.Silu)


class Modulate(Stage):

    def __init__(self, core, x, h, mod, b_mod):
        super().__init__(core)
        self.x, self.h, self.mod, self.b_mod = x, h, mod, b_mod
        self.s_dve = Steps(core.dve, "mod", 1)

    def apply(self, eng, parity):
        for k in range(parity, KT, 2):
            for which, a, b in ((1, 0, CTX), (0, CTX, TOK2)):
                scale, shift = self.mod[:, KT + k, which:which + 1], self.mod[:, k, which:which + 1]
                if parity == 0:
                    eng.activation(self.h[:, k, a:b], self.x[:, k, a:b], ACT.Identity, bias=shift, scale=scale)
                else:
                    eng.tensor_scalar(self.h[:, k, a:b], self.x[:, k, a:b], scale, shift, ALU.mult, ALU.add)

    def run_act(self, act):
        act.wait_ge(self.s_dve.sem, self.s_dve.at(0, "mod"))
        self.apply(act, 0)

    def run_dve(self, dve):
        dve.tensor_tensor(self.mod, self.mod, self.b_mod.unsqueeze(2).broadcast_to([P, 3 * KT, 2]), ALU.add)
        dve.drain()
        dve.tensor_scalar(self.mod[:, KT:2 * KT, :], self.mod[:, KT:2 * KT, :], 1.0, None, ALU.add)
        dve.drain().then_inc(self.s_dve.sem, 1)
        self.apply(dve, 1)


class Residual(Stage):

    def __init__(self, core, x, y, mod, parts):
        super().__init__(core)
        self.x, self.y, self.mod, self.parts = x, y, mod, parts
        self.s_act = Steps(core.act, [f"g{k}" for k in range(KT)], 1)

    def run_act(self, act):
        for k in range(KT):
            for which, a, b in self.parts:
                ins = act.activation(self.y[:, k, a:b], self.y[:, k, a:b], ACT.Copy, scale=self.mod[:, 2 * KT + k, which:which + 1])
            ins.then_inc(self.s_act.sem, 1)

    def run_dve(self, dve):
        for k in range(KT):
            dve.wait_ge(self.s_act.sem, self.s_act.at(0, f"g{k}"))
            dve.scalar_tensor_tensor(out=self.x[:, k, :], in0=self.x[:, k, :], scalar=ALPHA, in1=self.y[:, k, :],
                                     op0=ALU.mult, op1=ALU.add)


T3 = [(0, 512), (512, 1024), (1024, TOK2)]
RT = 3
SEGS = ((0, 1, CTX), (CTX, CTX + 3, SEQ))
RAW = TOK2 + 4
NCH = TOK2 // P
RW = ["R0", "Q0", "K0", "B0", "R1", "Q1", "K1", "B1", "V", "bonus"]


class RwkvPrep(Stage):

    def __init__(self, core, proj, par, low, low_src, rw, fac, areas):
        super().__init__(core)
        self.proj, self.par, self.low, self.low_src, self.rw, self.fac = proj, par, low, low_src, rw, fac
        names = ["raw0", "raw1", "raw2", "r", "k", "v", "kk", "sq", "L", "sw", "F", "E", "ic", "kd", "bd", "xR", "xQ", "xK", "ks", "one"]
        self.b = {}
        for start, end in areas:
            while names and start + RAW <= end:
                self.b[names.pop(0)] = core.region(start, RAW)
                start += RAW
        assert not names, names
        for n in self.b:
            if not n.startswith("raw"):
                self.b[n] = self.b[n][:, 0:TOK2]
        self.in_base = [core.moved[i].planned for i in range(4)]
        self.out_base = core.moved[4].planned
        for i in range(3):
            core.moved[i].planned += 32 * (RT + (1 if i == 0 else 0))
        core.moved[3].planned += 16
        core.moved[4].planned += 16 * RT * 10
        self.out_end = core.moved[4].planned
        self.s_pool = Steps(core.pool, "pads", 1)
        self.s_ld = Steps(core.dve, "L0 fix", 1)
        self.s_la = Steps(core.act, "L1", 1)
        self.s_pe = Steps(core.pe, "ksum zw0 za0 zw1 za1 bsum", RT)
        self.s_act = Steps(core.act, "sq kstd sw0 ic0 x0 sw1 ic1 x1", RT)
        self.s_dve = Steps(core.dve, "conv kkr kmax kk c0 out0 c1 out1 bon bonus", RT)

    def run_pool(self, pool):
        b = self.b
        for i in range(3):
            for a, n in ((0, 1), (CTX + 1, 2), (RAW - 1, 1)):
                pool.memset(b[f"raw{i}"][:, a:a + n], 0.0)
        pool.memset(b["one"], 1.0)
        pool.drain()
        pool.memset(b["one"].rearrange("p (c t) -> p c t", t=P)[:, :, 0:1], 0.0)
        pool.drain().then_inc(self.s_pool.sem, 1)

        def load(i, tile):
            src = self.proj[tile * P:(tile + 1) * P, :]
            for t, at, n in SEGS:
                pool.dma_start(b[f"raw{i}"][:, at:at + n], src[:, t:t + n]).then_inc(self.c.moved[i].sem, 16)

        pool.dma_start(self.low, self.low_src).then_inc(self.c.moved[3].sem, 16)
        load(0, 9)
        pool.wait_ge(self.s_ld.sem, self.s_ld.at(0, "L0"))
        for j in range(RT):
            if j:
                pool.wait_ge(self.s_dve.sem, self.s_dve.at(j - 1, "conv"))
            for i in range(3):
                load(i, 3 * i + j)
            out = lambda name, src: pool.dma_start(self.rw[name][j * P:(j + 1) * P, :], src).then_inc(self.c.moved[4].sem, 16)
            pool.wait_ge(self.s_dve.sem, self.s_dve.at(j, "conv"))
            out("V", b["v"])
            for d in range(2):
                pool.wait_ge(self.s_dve.sem, self.s_dve.at(j, f"out{d}"))
                for name, x in (("R", "xR"), ("Q", "xQ"), ("K", "kd"), ("B", "bd")):
                    out(f"{name}{d}", b[x])
            pool.wait_ge(self.s_dve.sem, self.s_dve.at(j, "bonus"))
            out("bonus", b["ks"])
        pool.wait_ge(self.c.moved[4].sem, self.out_end)

    def run_pe(self, pe):
        b, E, A, Dv, ps = self.b, self.s_pe, self.s_act, self.s_dve, self.c.psum

        def row(bank, lhs, rhs):
            for s, (x, y) in enumerate(T3):
                ins = pe.matmul(ps[:, bank + s, 0:y - x], lhs, rhs[:, x:y], start=True, stop=True)
            return ins

        pe.wait_ge(self.c.moved[3].sem, self.in_base[3] + 16)
        pe.wait_ge(self.s_la.sem, self.s_la.at(0, "L1"))
        for j in range(RT):
            pe.wait_ge(A.sem, A.at(j, "sq"))
            if j:
                pe.wait_ge(Dv.sem, Dv.at(j - 1, "bonus"))
            row(0, self.c.const("block_ones"), b["sq"]).then_inc(E.sem, 1)
            pe.wait_ge(Dv.sem, Dv.at(j, "kmax"))
            for d in range(2):
                if d:
                    pe.wait_ge(A.sem, A.at(j, "sw0"))
                row(0, self.low[:, d * 384 + j * P:d * 384 + (j + 1) * P], b["L"]).then_inc(E.sem, 1)
                if d:
                    pe.wait_ge(A.sem, A.at(j, "ic0"))
                row(3, self.low[:, (2 + d) * 384 + j * P:(2 + d) * 384 + (j + 1) * P], b["L"]).then_inc(E.sem, 1)
            pe.wait_ge(A.sem, A.at(j, "sw1"))
            pe.wait_ge(Dv.sem, Dv.at(j, "bon"))
            row(0, self.c.const("block_ones"), b["kd"]).then_inc(E.sem, 1)

    def run_act(self, act):
        b, E, A, Dv, ps = self.b, self.s_pe, self.s_act, self.s_dve, self.c.psum
        flat = lambda bank: ps[:, bank:bank + 3, :].rearrange("p a b -> p (a b)")[:, 0:TOK2]
        act.wait_ge(self.s_ld.sem, self.s_ld.at(0, "L0"))
        act.activation(b["L"][0:64, :], b["L"][0:64, :], ACT.Tanh).then_inc(self.s_la.sem, 1)
        for j in range(RT):
            act.wait_ge(Dv.sem, Dv.at(j, "kkr"))
            act.activation(b["sq"], b["kk"], ACT.Square).then_inc(A.sem, 1)
            act.wait_ge(Dv.sem, Dv.at(j, "kmax"))
            act.activation(b["sq"], b["sq"], ACT.Sqrt).then_inc(A.sem, 1)
            for d in range(2):
                act.wait_ge(E.sem, E.at(j, f"zw{d}"))
                if d:
                    act.wait_ge(Dv.sem, Dv.at(j, "out0"))
                act.activation(b["sw"], flat(0), ACT.Sigmoid, bias=self.par("decay_w0", d * RT + j)).then_inc(A.sem, 1)
                act.wait_ge(E.sem, E.at(j, f"za{d}"))
                act.activation(b["ic"], flat(3), ACT.Sigmoid, bias=self.par("iclr_a0", d * RT + j)).then_inc(A.sem, 1)
                act.wait_ge(Dv.sem, Dv.at(j, f"c{d}"))
                act.wait_ge(self.c.moved[4].sem, self.out_base + 16 * (10 * j + (5 if d else 0)))
                for x, src, sign in ((("xR", "F", 1.0), ("xQ", "E", 1.0), ("xK", "F", -1.0)) if d == 0 else
                                     (("xR", "E", -1.0), ("xQ", "F", -1.0), ("xK", "E", 1.0))):
                    act.activation(b[x], b[src], ACT.Exp, scale=sign)
                f = self.fac[:, d, j]
                act.activation(f, f, ACT.Exp)
                act.drain().then_inc(A.sem, 1)

    def conv(self, dve, raw, dst, tile, out_rows=slice(0, P)):
        for w in range(3):
            if w:
                dve.drain()
            for t, at, n in SEGS:
                src = raw[:, at - 1 + w:at - 1 + w + n]
                tap = self.par("rwkv_conv", w * 10 + tile)
                if w == 0:
                    dve.tensor_scalar(dst[:, t:t + n], src, tap, None, ALU.mult)
                else:
                    dve.scalar_tensor_tensor(out=dst[:, t:t + n], in0=src, scalar=tap, in1=dst[:, t:t + n], op0=ALU.mult, op1=ALU.add)

    def run_dve(self, dve):
        b, E, A, Dv, ps = self.b, self.s_pe, self.s_act, self.s_dve, self.c.psum
        flat = lambda bank: ps[:, bank:bank + 3, :].rearrange("p a b -> p (a b)")[:, 0:TOK2]
        ch = lambda a: a.rearrange("p (c t) -> p c t", t=P)
        dve.wait_ge(self.s_pool.sem, self.s_pool.at(0, "pads"))
        dve.wait_ge(self.c.moved[0].sem, self.in_base[0] + 32)
        self.conv(dve, b["raw0"], b["L"], 9)
        dve.drain().then_inc(self.s_ld.sem, 1)
        for j in range(RT):
            dve.tensor_scalar(self.par("one_less_k_a", j), self.par("k_a", j), -1.0, 1.0, ALU.mult, ALU.add)
        dve.drain().then_inc(self.s_ld.sem, 1)
        for j in range(RT):
            for i, x in enumerate("rkv"):
                dve.wait_ge(self.c.moved[i].sem, self.in_base[i] + 32 * (j + 1) + (32 if i == 0 else 0))
                if i == 0:
                    dve.wait_ge(self.c.moved[4].sem, self.out_base + 160 * j)
                self.conv(dve, b[f"raw{i}"], b[x], 3 * i + j)
            dve.drain().then_inc(Dv.sem, 1)
            dve.tensor_scalar(b["kk"], b["k"], self.par("k_k", j), None, ALU.mult).then_inc(Dv.sem, 1)
            dve.wait_ge(E.sem, E.at(j, "ksum"))
            dve.tensor_scalar(b["sq"], flat(0), 1e-12, None, ALU.max).then_inc(Dv.sem, 1)
            dve.wait_ge(A.sem, A.at(j, "kstd"))
            dve.reciprocal(b["sq"], b["sq"])
            dve.drain()
            dve.tensor_tensor(b["kk"], b["kk"], b["sq"], ALU.mult)
            dve.drain().then_inc(Dv.sem, 1)
            for d in range(2):
                dve.wait_ge(A.sem, A.at(j, f"sw{d}"))
                dve.tensor_scalar(b["sw"], b["sw"], -DECAY_MAX, None, ALU.mult)
                dve.drain()
                dve.tensor_tensor_scan(b["F"], b["one"], b["sw"], 0.0, ALU.mult, ALU.add)
                dve.drain()
                f = self.fac[:, d, j]
                mid = ch(b["F"])[:, :, P // 2 - 1:P // 2]
                dve.tensor_tensor(b["E"], b["F"], b["sw"], ALU.subtract)
                dve.tensor_copy(f[:, :, 0], mid.rearrange("p c o -> p (c o)"))
                dve.drain()
                fm = f[:, :, 0:1].broadcast_to([P, NCH, P])
                dve.tensor_tensor(ch(b["E"]), ch(b["E"]), fm, ALU.subtract)
                dve.tensor_tensor(ch(b["F"]), ch(b["F"]), fm, ALU.subtract)
                dve.drain()
                dve.tensor_copy(f[:, :, 1], ch(b["F"])[:, :, P - 1])
                dve.drain().then_inc(Dv.sem, 1)
                dve.wait_ge(A.sem, A.at(j, f"x{d}"))
                dve.tensor_scalar(b["kd"], b["ic"], self.par("k_a", j), self.par("one_less_k_a", j), ALU.mult, ALU.add)
                dve.tensor_tensor(b["bd"], b["kk"], b["ic"], ALU.mult)
                dve.tensor_tensor(b["xR"], b["r"], b["xR"], ALU.mult)
                dve.tensor_tensor(b["xQ"], b["kk"], b["xQ"], ALU.mult)
                dve.drain()
                dve.tensor_tensor(b["kd"], b["kd"], b["k"], ALU.mult)
                dve.tensor_tensor(b["bd"], b["bd"], b["xK"], ALU.mult)
                dve.drain()
                if d == 0:
                    dve.tensor_copy(b["ks"], b["kd"])
                else:
                    dve.tensor_tensor(b["ks"], b["ks"], b["kd"], ALU.add)
                dve.drain()
                dve.tensor_tensor(b["kd"], b["kd"], b["xK"], ALU.mult)
                dve.drain().then_inc(Dv.sem, 1)
            dve.tensor_tensor(b["ks"], b["ks"], b["r"], ALU.mult)
            dve.drain()
            dve.wait_ge(self.c.moved[4].sem, self.out_base + 160 * j + 144)
            dve.tensor_scalar(b["kd"], b["ks"], self.par("r_k", j), None, ALU.mult).then_inc(Dv.sem, 1)
            dve.wait_ge(E.sem, E.at(j, "bsum"))
            dve.tensor_tensor(b["ks"], flat(0), b["v"], ALU.mult).then_inc(Dv.sem, 1)


def over3(m):
    return m.unsqueeze(1).broadcast_to([P, 3, P])


def tri(a):
    return a.rearrange("p (h t) -> p h t", h=3)


class Rwkv(Stage):

    def __init__(self, core, rw, fac, y, areas):
        super().__init__(core)
        self.rw, self.fac, self.y = rw, fac, y
        b = self.b = {}
        names = [f"{x}{d}" for d in range(2) for x in "RQKBV"] + [f"t{x}{d}" for d in range(2) for x in "VKB"]
        names += [f"{x}{g}" for g in range(4) for x in ("A", "AT", "QK", "RK", "RB", "X", "XT", "Y", "M0_", "M1_")]
        names += [f"{x}{d}" for d in range(2) for x in ("H", "Hc", "G", "U", "O", "TO")]
        for start, end in areas:
            while names and start + 384 <= end:
                b[names.pop(0)] = core.region(start, 384)
                start += 384
        assert not names, names
        self.fc = core.region(areas[-1][1], 2, RT, 3)
        prod = [f"t{x}{d}" for d in range(2) for x in "VKB"]
        prod += [f"{x}{g}" for g in range(4) for x in ("A", "AT", "QK", "RK", "RB")]
        for l in range(1, LEVELS):
            prod += [f"y{l}_{g}" for g in range(4)]
            for g in range(4):
                prod += [f"{x}{l}_{g}" for x in ("x", "xT") if self.need(l, g, x)]
        prod += [f"{x}{d}" for x in ("G", "U", "O", "H", "TO") for d in range(2)]
        self.prod = prod
        self.on_act = {p: p[0] == "t" or p[0] == "y" or p[0] in "GUO" or p[:2] == "TO" for p in prod}
        self.in_base = core.moved[0].planned
        core.moved[0].planned += 160 * NCH
        self.out_base = core.moved[1].planned
        core.moved[1].planned += 32 * NCH
        self.out_end = core.moved[1].planned
        self.s_pool = Steps(core.pool, ["fac"] + [f"{x}{g}" for g in range(4) for x in ("X", "XT")]
                            + [f"m{l}_{g}" for l in range(1, LEVELS) for g in range(4)], NCH)
        self.s_pe = Steps(core.pe, prod, NCH)
        self.s_act = Steps(core.act, [p for p in prod if self.on_act[p]], NCH)
        self.s_dve = Steps(core.dve, ["Hc0", "Hc1"] + [p for p in prod if not self.on_act[p]], NCH)

    def need(self, l, g, x):
        return l < LEVELS - 1 or x == ("xT" if g < 2 else "x")

    def bank(self, p):
        return self.c.psum[:, self.prod.index(p) % 8, 0:384]

    def run_pool(self, pool):
        b, s, E, A, Dv = self.b, self.s_pool, self.s_pe, self.s_act, self.s_dve

        def chunk(n, cb):
            pool.wait_ge(E.sem, E.before(n, 0))
            pool.wait_ge(Dv.sem, Dv.before(n, 0))
            for d, c in ((0, n), (1, cb)):
                for x in "RQKBV":
                    src = self.rw[x + str(d) if x != "V" else "V"].rearrange("(j p) t -> p j t", p=P)[:, :, ds(c * P, P)]
                    pool.dma_start(tri(b[f"{x}{d}"]), src).then_inc(self.c.moved[0].sem, 16)
            for d, c in ((0, n), (1, cb)):
                f = self.fac[:, d].rearrange("p j c x -> p j (c x)")
                pool.tensor_copy(self.fc[:, d, :, 2], f[:, :, ds(c * 2 + d, 1)].rearrange("p j o -> p (j o)"))
            pool.drain()
            pool.tensor_tensor(self.fc[:, :, :, 0], self.fc[:, :, :, 2], self.fc[:, :, :, 1], ALU.mult)
            pool.drain()
            for d, c in ((0, n), (1, cb)):
                f = self.fac[:, d].rearrange("p j c x -> p j (c x)")
                pool.tensor_copy(self.fc[:, d, :, 1], f[:, :, ds(c * 2 + (1 - d), 1)].rearrange("p j o -> p (j o)"))
            pool.drain().then_inc(s.sem, 1)
            for g in range(4):
                for x, src, lev in (("X", "A", "lev"), ("XT", "AT", "levT")):
                    pool.wait_ge(Dv.sem, Dv.at(n, f"{src}{g}"))
                    pool.tensor_tensor(tri(b[f"{x}{g}"]), tri(b[f"{src}{g}"]), over3(self.c.const(lev, 0)), ALU.mult)
                    pool.drain()
                    pool.tensor_tensor(tri(b[f"{x}{g}"]), over3(self.c.const("ident")), tri(b[f"{x}{g}"]),
                                       ALU.subtract).then_inc(s.sem, 1)
            for l in range(1, LEVELS):
                for g in range(4):
                    if l > 2:
                        pool.wait_ge(E.sem, E.at(n, f"y{l - 2}_{g}"))
                    pool.tensor_tensor(tri(b[f"M{l % 2}_{g}"]), tri(b[f"AT{g}"]), over3(self.c.const("levT", l)),
                                       ALU.mult).then_inc(s.sem, 1)
            pool.wait_ge(A.sem, A.at(n, "TO1"))
            pool.tensor_tensor(self.fc[:, 0, :, 2], self.fc[:, 0, :, 2], self.fc[:, 0, :, 2], ALU.mult)
            pool.drain()
            for d, c in ((0, n), (1, cb)):
                dst = self.y[d].rearrange("(j p) t -> p j t", p=P)[:, :, ds(c * P, P)]
                pool.dma_start(dst, tri(b[f"TO{d}"])).then_inc(self.c.moved[1].sem, 16)

        pool.memset(self.fc[:, :, :, :], 1.0)
        pool.drain()
        nctx = CTX // P
        with pool.Fori(0, nctx) as n:
            chunk(n, (nctx - 1) - n)
        with pool.Fori(nctx, NCH) as n:
            chunk(n, (NCH + nctx - 1) - n)
        pool.wait_ge(self.c.moved[1].sem, self.out_end)

    def run_pe(self, pe):
        b, s, O, A, Dv = self.b, self.s_pe, self.s_pool, self.s_act, self.s_dve
        N = len(self.prod)
        ident = self.c.const("ident")

        with pe.Fori(0, NCH) as n:
            def start(p):
                i = self.prod.index(p)
                old = self.prod[i - 8] if i >= 8 else None
                if old:
                    st = A if self.on_act[old] else Dv
                    pe.wait_ge(st.sem, st.at(n, old))
                return self.bank(p)

            def done(ins):
                ins.then_inc(s.sem, 1)

            pe.wait_ge(self.c.moved[0].sem, (n + 1) * 160 + self.in_base)
            pe.wait_ge(A.sem, A.before(n, 0))
            pe.wait_ge(Dv.sem, Dv.before(n, 0))
            for d in range(2):
                for x in "VKB":
                    out = start(f"t{x}{d}")
                    for j in range(3):
                        ins = pe.transpose(out[:, j * P:(j + 1) * P], b[f"{x}{d}"][:, j * P:(j + 1) * P], ident)
                    done(ins)

            def head(name, h):
                p = h % 2
                return b[name][64 * p:64 * p + 64, h // 2 * P:(h // 2 + 1) * P]

            for g in range(4):
                d = g // 2
                for p, l, r in ((f"A{g}", "QB"[d], "BQ"[d]), (f"AT{g}", "BQ"[d], "QB"[d]), (f"QK{g}", "K", "Q"),
                                (f"RK{g}", "K", "R"), (f"RB{g}", "B", "R")):
                    out = start(p)
                    for x in range(3):
                        h = 2 * x + g % 2
                        ins = pe.matmul(out[:, x * P:(x + 1) * P], head(f"{l}{d}", h), head(f"{r}{d}", h), start=True, stop=True)
                    done(ins)
            sl = lambda name, x: b[name][:, x * P:(x + 1) * P]
            for l in range(1, LEVELS):
                for g in range(4):
                    pe.wait_ge(O.sem, O.at(n, f"m{l}_{g}"))
                    if l > 1:
                        pe.wait_ge(Dv.sem, Dv.at(n, f"xT{l - 1}_{g}"))
                    out = start(f"y{l}_{g}")
                    for x in range(3):
                        ins = pe.matmul(out[:, x * P:(x + 1) * P], sl(f"M{l % 2}_{g}", x), sl(f"X{g}", x), start=True, stop=True)
                    done(ins)
                for g in range(4):
                    pe.wait_ge(A.sem, A.at(n, f"y{l}_{g}"))
                    for kind in ("x", "xT"):
                        if self.need(l, g, kind):
                            out = start(f"{kind}{l}_{g}")
                            for x in range(3):
                                lhs, rhs = (sl(f"XT{g}", x), sl(f"Y{g}", x)) if kind == "x" else (sl(f"Y{g}", x), sl(f"XT{g}", x))
                                ins = pe.matmul(out[:, x * P:(x + 1) * P], lhs, rhs, start=True, stop=True)
                            done(ins)
            inv = lambda d, h: sl(("XT" if d == 0 else "X") + str(2 * d + h % 2), h // 2)
            mat = lambda name, d, h: sl(f"{name}{2 * d + h % 2}", h // 2)
            v = lambda name, d, h: b[f"{name}{d}"][:, h * 64:(h + 1) * 64]
            pair = lambda name, d, j: b[f"{name}{d}"][:, j * P:(j + 1) * P]
            for d in range(2):
                pe.wait_ge(Dv.sem, Dv.at(n, f"Hc{d}"))
                out = start(f"G{d}")
                for j in range(3):
                    pe.matmul(out[:, j * P:(j + 1) * P], pair("Q", d, j), pair("Hc", d, j), start=True, stop=False, skip_group_check=True)
                    for h in (2 * j, 2 * j + 1):
                        ins = pe.matmul(out[:, h * 64:(h + 1) * 64], mat("QK", d, h), v("tV", d, h), start=False, stop=True, skip_group_check=True)
                done(ins)
            for d in range(2):
                pe.wait_ge(A.sem, A.at(n, f"G{d}"))
                pe.wait_ge(Dv.sem, Dv.at(n, f"{'xT' if d == 0 else 'x'}{LEVELS - 1}_{2 * d + 1}"))
                out = start(f"U{d}")
                for h in range(6):
                    ins = pe.matmul(out[:, h * 64:(h + 1) * 64], inv(d, h), v("G", d, h), start=True, stop=True)
                done(ins)
            for d in range(2):
                pe.wait_ge(A.sem, A.at(n, f"U{d}"))
                out = start(f"O{d}")
                for j in range(3):
                    pe.matmul(out[:, j * P:(j + 1) * P], pair("R", d, j), pair("Hc", d, j), start=True, stop=False, skip_group_check=True)
                    for h in (2 * j, 2 * j + 1):
                        pe.matmul(out[:, h * 64:(h + 1) * 64], mat("RK", d, h), v("tV", d, h), start=False, stop=False, skip_group_check=True)
                        ins = pe.matmul(out[:, h * 64:(h + 1) * 64], mat("RB", d, h), v("U", d, h), start=False, stop=True, skip_group_check=True)
                done(ins)
            for d in range(2):
                out = start(f"H{d}")
                for j in range(3):
                    pe.matmul(out[:, j * P:(j + 1) * P], pair("tK", d, j), pair("tV", d, j), start=True, stop=False)
                    ins = pe.matmul(out[:, j * P:(j + 1) * P], pair("tB", d, j), pair("U", d, j), start=False, stop=True)
                done(ins)
            for d in range(2):
                pe.wait_ge(A.sem, A.at(n, f"O{d}"))
                out = start(f"TO{d}")
                for j in range(3):
                    ins = pe.transpose(out[:, j * P:(j + 1) * P], pair("O", d, j), ident)
                done(ins)

    def run_act(self, act):
        b, s, E = self.b, self.s_act, self.s_pe
        with act.Fori(0, NCH) as n:
            act.wait_ge(self.c.moved[1].sem, n * 32 + self.out_base)
            for p in self.prod:
                if not self.on_act[p]:
                    continue
                act.wait_ge(E.sem, E.at(n, p))
                dst = b[f"Y{p[-1]}"] if p[0] == "y" else b[p]
                if p[0] == "U":
                    ins = act.activation(dst, self.bank(p), ACT.Copy, scale=-1.0)
                else:
                    ins = act.copy(dst, self.bank(p))
                ins.then_inc(s.sem, 1)

    def run_dve(self, dve):
        b, s, E, O = self.b, self.s_dve, self.s_pe, self.s_pool
        masks = {"A": ("strict_low", "strict_low"), "AT": ("strict_up", "strict_up"), "QK": ("strict_up", "strict_low"),
                 "RK": ("upper", "lower"), "RB": ("upper", "lower")}
        for d in range(2):
            dve.memset(b[f"H{d}"], 0.0)
        dve.drain()
        with dve.Fori(0, NCH) as n:
            dve.wait_ge(O.sem, O.at(n, "fac"))
            for d in range(2):
                for j in range(3):
                    ins = dve.tensor_scalar(b[f"Hc{d}"][:, j * P:(j + 1) * P], b[f"H{d}"][:, j * P:(j + 1) * P],
                                            self.fc[:, d, j, 0:1], None, ALU.mult)
                ins.then_inc(s.sem, 1)
            for p in self.prod:
                if self.on_act[p]:
                    continue
                dve.wait_ge(E.sem, E.at(n, p))
                if p[0] == "x":
                    dst = b[("X" if p[1] != "T" else "XT") + p[-1]]
                    if "1_" in p:
                        dve.wait_ge(O.sem, O.at(n, ("X" if p[1] != "T" else "XT") + p[-1]))
                    dve.tensor_tensor(dst, dst, self.bank(p), ALU.subtract).then_inc(s.sem, 1)
                elif p[0] == "H":
                    dve.tensor_tensor(tri(b[p]), tri(self.bank(p)), over3(self.c.const("block_ones")), ALU.mult)
                    dve.drain()
                    dve.tensor_tensor(b[p], b[p], b["Hc" + p[-1]], ALU.add)
                    dve.drain().then_inc(s.sem, 1)
                else:
                    kind, g = p[:-1], int(p[-1])
                    dve.tensor_tensor(tri(b[p]), tri(self.bank(p)), over3(self.c.const(masks[kind][g // 2])), ALU.mult).then_inc(s.sem, 1)


class RwkvOut(Stage):

    def __init__(self, core, y, bonus, gate, mix, par, at):
        super().__init__(core)
        self.y, self.bonus, self.gate, self.mix, self.par = y, bonus, gate, mix, par
        R = core.region
        self.a, self.b2, self.bo, self.g, self.t, self.m = [R(at + i * TOK2, TOK2) for i in range(6)]
        self.base = core.moved[0].planned
        core.moved[0].planned += 64 * RT
        self.s_pe = Steps(core.pe, "mean var", RT)
        self.s_act = Steps(core.act, "mean sq std gate", RT)
        self.s_dve = Steps(core.dve, "sum cen out", RT)

    def run_pool(self, pool):
        for j in range(RT):
            pool.wait_ge(self.s_dve.sem, self.s_dve.before(j, 0))
            for dst, src in ((self.a, self.y[0]), (self.b2, self.y[1]), (self.bo, self.bonus), (self.g, self.gate)):
                pool.dma_start(dst, src[j * P:(j + 1) * P, :]).then_inc(self.c.moved[0].sem, 16)

    def run_pe(self, pe):
        for j in range(RT):
            for bank, x, st, name in ((0, self.a, self.s_dve, "sum"), (3, self.t, self.s_act, "sq")):
                pe.wait_ge(st.sem, st.at(j, name))
                for s, (u, v) in enumerate(T3):
                    ins = pe.matmul(self.c.psum[:, bank + s, 0:v - u], self.c.const("block_ones"), x[:, u:v], start=True, stop=True)
                ins.then_inc(self.s_pe.sem, 1)

    def run_act(self, act):
        flat = lambda bank: self.c.psum[:, bank:bank + 3, :].rearrange("p a b -> p (a b)")[:, 0:TOK2]
        for j in range(RT):
            act.wait_ge(self.s_pe.sem, self.s_pe.at(j, "mean"))
            act.wait_ge(self.s_dve.sem, self.s_dve.before(j, 0))
            act.activation(self.m, flat(0), ACT.Copy, scale=1.0 / 64).then_inc(self.s_act.sem, 1)
            act.wait_ge(self.s_dve.sem, self.s_dve.at(j, "cen"))
            act.activation(self.t, self.a, ACT.Square).then_inc(self.s_act.sem, 1)
            act.wait_ge(self.s_pe.sem, self.s_pe.at(j, "var"))
            act.activation(self.t, flat(3), ACT.Sqrt, scale=1.0 / 64, bias=GN_EPS).then_inc(self.s_act.sem, 1)
            act.activation(self.g, self.g, ACT.Silu).then_inc(self.s_act.sem, 1)

    def run_dve(self, dve):
        for j in range(RT):
            dve.wait_ge(self.c.moved[0].sem, self.base + 64 * (j + 1))
            dve.tensor_tensor(self.a, self.a, self.b2, ALU.add).then_inc(self.s_dve.sem, 1)
            dve.wait_ge(self.s_act.sem, self.s_act.at(j, "mean"))
            dve.tensor_tensor(self.a, self.a, self.m, ALU.subtract).then_inc(self.s_dve.sem, 1)
            dve.wait_ge(self.s_act.sem, self.s_act.at(j, "gate"))
            dve.reciprocal(self.t, self.t)
            dve.drain()
            dve.scalar_tensor_tensor(out=self.a, in0=self.a, scalar=self.par("gn_g", j), in1=self.t, op0=ALU.mult, op1=ALU.mult)
            dve.drain()
            dve.scalar_tensor_tensor(out=self.a, in0=self.a, scalar=self.par("gn_b", j), in1=self.bo, op0=ALU.add, op1=ALU.add)
            dve.drain()
            dve.tensor_tensor(self.mix[:, j, :], self.a, self.g, ALU.mult)
            dve.drain().then_inc(self.s_dve.sem, 1)


class GqaPrep(Stage):

    def __init__(self, core, proj, kx, vx, cos, sin, rope_src, par, at):
        super().__init__(core)
        self.proj, self.kx, self.vx, self.par = proj, kx, vx, par
        R = core.region
        self.cos, self.sin = R(at, SEQ), R(at + SEQ, SEQ)
        self.cos_src, self.sin_src = cos, sin
        at += 2 * SEQ
        self.x, self.sq, self.rot = [R(at + i * TOK2, TOK2) for i in range(3)]
        self.base = core.moved[0].planned
        core.moved[0].planned += 64
        self.tab = core.moved[1].planned
        core.moved[1].planned += 32
        self.out = core.moved[2].planned
        core.moved[2].planned += 16 * (3 + 6 + 6)
        self.s_pe = Steps(core.pe, "sum rot", 4)
        self.s_act = Steps(core.act, "sq std", 4)
        self.s_dve = Steps(core.dve, "norm out", 4)

    def run_pool(self, pool):
        pool.dma_start(self.cos, self.cos_src).then_inc(self.c.moved[1].sem, 16)
        pool.dma_start(self.sin, self.sin_src).then_inc(self.c.moved[1].sem, 16)
        for g in range(2):
            for r in range(3):
                pool.dma_start(self.vx[(3 * g + r) * 64:(3 * g + r + 1) * 64, :],
                               self.proj[17 * P + 64 * g:17 * P + 64 * g + 64, :]).then_inc(self.c.moved[2].sem, 16)
        for j in range(4):
            rows = self.proj[(13 + j) * P:(14 + j) * P, :]
            if j:
                pool.wait_ge(self.c.moved[2].sem, self.out + 96 + 16 * j)
            pool.dma_start(self.x, rows).then_inc(self.c.moved[0].sem, 16)
            pool.wait_ge(self.s_dve.sem, self.s_dve.at(j, "out"))
            if j < 3:
                pool.dma_start(rows, self.x).then_inc(self.c.moved[2].sem, 16)
            else:
                for g in range(2):
                    for r in range(3):
                        pool.dma_start(self.kx[(3 * g + r) * 64:(3 * g + r + 1) * 64, :],
                                       self.x[64 * g:64 * g + 64, :]).then_inc(self.c.moved[2].sem, 16)
        pool.wait_ge(self.c.moved[2].sem, self.out + 240)

    def run_pe(self, pe):
        for j in range(4):
            pe.wait_ge(self.s_act.sem, self.s_act.at(j, "sq"))
            for s, (u, v) in enumerate(T3):
                ins = pe.matmul(self.c.psum[:, s, 0:v - u], self.c.const("block_ones"), self.sq[:, u:v], start=True, stop=True)
            ins.then_inc(self.s_pe.sem, 1)
            pe.wait_ge(self.s_dve.sem, self.s_dve.at(j, "norm"))
            for s in range(2):
                ins = pe.matmul(self.c.psum[:, 3 + s, :], self.c.const("rope"), self.x[:, CTX + 512 * s:CTX + 512 * s + 512],
                                start=True, stop=True)
            ins.then_inc(self.s_pe.sem, 1)

    def run_act(self, act):
        flat = self.c.psum[:, 0:3, :].rearrange("p a b -> p (a b)")[:, 0:TOK2]
        for j in range(4):
            act.wait_ge(self.c.moved[0].sem, self.base + 16 * (j + 1))
            act.activation(self.sq, self.x, ACT.Square).then_inc(self.s_act.sem, 1)
            act.wait_ge(self.s_pe.sem, self.s_pe.at(j, "sum"))
            act.activation(self.sq, flat, ACT.Sqrt, scale=1.0 / 64, bias=EPS).then_inc(self.s_act.sem, 1)

    def run_dve(self, dve):
        dve.wait_ge(self.c.moved[1].sem, self.tab + 32)
        for j in range(4):
            dve.wait_ge(self.s_act.sem, self.s_act.at(j, "std"))
            dve.reciprocal(self.sq, self.sq)
            dve.drain()
            dve.scalar_tensor_tensor(out=self.x, in0=self.x, scalar=self.par("q_norm" if j < 3 else "k_norm", 0), in1=self.sq,
                                     op0=ALU.mult, op1=ALU.mult).then_inc(self.s_dve.sem, 1)
            dve.wait_ge(self.s_pe.sem, self.s_pe.at(j, "rot"))
            lat = self.x[:, CTX:TOK2]
            dve.tensor_tensor(self.rot[:, 0:SEQ], self.c.psum[:, 3:5, :].rearrange("p a b -> p (a b)"), self.sin, ALU.mult)
            dve.drain()
            dve.tensor_tensor(lat, lat, self.cos, ALU.mult)
            dve.drain()
            dve.tensor_tensor(lat, lat, self.rot[:, 0:SEQ], ALU.add)
            dve.drain().then_inc(self.s_dve.sem, 1)


class GateTiles(Stage):

    def __init__(self, core, mix, tiles_rows, at, t0):
        super().__init__(core)
        self.mix, self.tr, self.t0 = mix, tiles_rows, t0
        self.g = core.region(at, 2, TOK2)
        self.base = [core.moved[i].planned for i in range(2)]
        for x in range(len(tiles_rows)):
            core.moved[x % 2].planned += 16
        n = len(tiles_rows)
        self.s_act = Steps(core.act, [f"g{x}" for x in range(n)], 1)
        self.s_dve = Steps(core.dve, [f"o{x}" for x in range(n)], 1)

    def run_pool(self, pool):
        for x, (k, rows) in enumerate(self.tr):
            if x >= 2:
                pool.wait_ge(self.s_dve.sem, self.s_dve.at(0, f"o{x - 2}"))
            pool.dma_start(self.g[:, x % 2, :], rows).then_inc(self.c.moved[x % 2].sem, 16)

    def run_act(self, act):
        for x in range(len(self.tr)):
            act.wait_ge(self.c.moved[x % 2].sem, self.base[x % 2] + 16 * (x // 2 + 1))
            act.activation(self.g[:, x % 2, :], self.g[:, x % 2, :], ACT.Silu).then_inc(self.s_act.sem, 1)

    def run_dve(self, dve):
        for x, (k, rows) in enumerate(self.tr):
            dve.wait_ge(self.s_act.sem, self.s_act.at(0, f"g{x}"))
            m = self.mix[:, k, self.t0:TOK2]
            dve.tensor_tensor(m, m, self.g[:, x % 2, self.t0:TOK2], ALU.mult).then_inc(self.s_dve.sem, 1)


GRID, WIN_R, WIN_C = 64, 8, 16
NA_ROWS = 10
NA_KEYS = NA_ROWS * GRID
NA_SLOTS = 18
NA_TAB = 19 * 127


def na_first(t):
    return min(max(2 * t - 4, 0), SEQ // GRID - NA_ROWS)


NA_KINDS = sorted({na_first(t) - 2 * t for t in range(SEQ // P)})


def na_masks():
    rows = SEQ // GRID
    out = np.full((P, len(NA_KINDS), NA_ROWS, GRID), NEG, np.float32)
    for t in range(SEQ // P):
        kind = NA_KINDS.index(na_first(t) - 2 * t)
        for p in range(P):
            r, c = 2 * t + p // GRID, p % GRID
            r0 = min(max(r - WIN_R // 2, 0), rows - WIN_R)
            c0 = min(max(c - WIN_C // 2, 0), GRID - WIN_C)
            out[p, kind, r0 - na_first(t):r0 - na_first(t) + WIN_R, c0:c0 + WIN_C] = 0.0
    return out.reshape(P, -1)


class NaBand(Stage):

    def __init__(self, core, pad, band):
        super().__init__(core)
        self.pad, self.band = pad, band
        core.moved[0].planned += 16
        self.end = core.moved[0].planned

    def run_pool(self, pool):
        pool.dma_start(self.band.rearrange("(h c i) -> h c i", h=4, c=GRID),
                       self.pad.unsqueeze(1).broadcast_to([4, GRID, NA_TAB])).then_inc(self.c.moved[0].sem, 16)
        pool.wait_ge(self.c.moved[0].sem, self.end)


PAR2 = {"b_mod": 24, "rwkv_conv": 30, "decay_w0": 6, "iclr_a0": 6, "k_k": 3, "k_a": 3, "one_less_k_a": 3, "r_k": 3,
        "gn_g": 3, "gn_b": 3, "q_norm": 1, "k_norm": 1, "ln_g": 8, "ln_b": 8}
PARAM2 = {}
_at = 0
for _name, _n in PAR2.items():
    PARAM2[_name] = (_at, _n)
    _at += _n
NPAR2 = _at


def second_block(nc, core, a, par_at, xT1):
    R = core.region
    at = par_at
    p2 = R(at, 2, NPAR2); at += 2 * NPAR2
    cond = R(at, KT, 2); at += 16
    scond = R(at, KT, 2); at += 16
    mod = R(at, 3 * KT, 2); at += 48
    fac_at = at
    fac = R(at, 2, RT, NCH * 2).rearrange("p d j (c x) -> p d j c x", x=2); at += 2 * RT * NCH * 2
    h = R(at, KT, TOK2)
    x = R(at + KT * TOK2, KT, TOK2)
    h_at, big, top = at, at + 2 * KT * TOK2, TOP
    dram = lambda name, *shape: nc.dram_tensor(name, shape, F32, kind="Internal").ap()
    proj = dram("proj2", 29 * P, TOK2)
    rw = {n: dram("rw_" + n, RT * P, TOK2) for n in RW}
    y_dir = [dram(f"rwkv_y{d}", RT * P, TOK2) for d in range(2)]
    kx, vx = dram("kx", RT * P, TOK2), dram("vx", RT * P, TOK2)
    band = dram("na_band", 4 * GRID * NA_TAB)
    kview = lambda w: w.rearrange("(k p) f -> p k f", p=P)

    CopyTiles(core, x[:, :, CTX:TOK2], xT1)
    LoadInputs(core, [(p2, a["params2"]), (cond, a["cond"])])
    LoadTokens(core, a["ctx_2"], CTX // P, x, 0, R(big, 2, D))
    CondVector(core, cond, scond)
    for l in range(2):
        last = l == 1
        par = lambda name, i=0, l=l: p2[:, l, PARAM2[name][0] + i:PARAM2[name][0] + i + 1]
        Gemm(core, [kview(a["w_mod_2"][l])], [(0, 0, KT)], [(0, 3 * KT, 0)], lambda k, n0, n1: scond[:, k, n0:n1], [(0, 2)],
             "keep", 4, mod.rearrange("p f w -> p (f w)")).close()
        Modulate(core, x, h, mod, p2[:, l, 0:24])
        Gemm(core, [kview(a["w_in_2"][l])], [(0, 0, KT)], [(0, 29, 0)], lambda k, n0, n1: h[:, k, n0:n1], T3, "store", 4,
             proj, R(big, 4, TOK2)).close()
        low = R(big, 4 * 384)
        RwkvPrep(core, proj, par, low, a["lowrank"][l], rw, fac, [(h_at, h_at + KT * TOK2), (big + 4 * 384, top)])
        Rwkv(core, rw, fac, y_dir, [(h_at, h_at + KT * TOK2), (big, top - 32)])
        RwkvOut(core, y_dir, rw["bonus"], proj[10 * P:13 * P, :], h, par, big)
        GqaPrep(core, proj, kx, vx, a["rope_cos"], a["rope_sin"], None, par, big)
        ctx_units = [] if last else [(q, [(0, CTX)]) for q in range(CTX // P)]
        units = ctx_units + [(CTX // P + t, [(0, TOK2)]) for t in range(SEQ // P)]
        row = lambda base, src=proj: (lambda it: src[ds(it * P + base * P, P), :])
        out_at = lambda tile: (lambda it, rows, q0, n: h[rows, tile:tile + 3, :].rearrange("p k t -> p (k t)")[:, ds(it * TOK2 + q0, n)])
        Attention(core, 3, TOK2, TOK2, units, None,
                  lambda it, s: [(s.q, row(13)(it)), (s.k, row(0, kx)(it)), (s.v, row(0, vx)(it))], out_at(3), big, [6])
        NaBand(core, a["rpb_pad"][l], band)
        masks = R(big, len(NA_KINDS), NA_KEYS)
        tab = R(big + len(NA_KINDS) * NA_KEYS, 2, NA_SLOTS * GRID)

        def na_loads(it, s):
            out = [(s.q, row(21)(it)), (s.k, row(23)(it)), (s.v, row(25)(it))]
            for j in range(2):
                for r in range(2):
                    src = bass.AP(band.tensor, it * (2 * GRID * NA_TAB) + (j * GRID * NA_TAB + 63 + (1 - r) * 127),
                                  [[NA_TAB - 1, GRID], [127, NA_SLOTS], [1, GRID]])
                    out.append((tab[64 * r:64 * r + 64, j, :].rearrange("p (e c) -> p e c", c=GRID), src))
            return out

        def na_bias(pool, j, t, dst, nctx=len(ctx_units)):
            if t < nctx:
                return pool.tensor_tensor(dst[:, 0:1], dst[:, 0:1], dst[:, 0:1], ALU.add)
            t -= nctx
            e0 = na_first(t) - 2 * t + 8
            kind = NA_KINDS.index(na_first(t) - 2 * t)
            return pool.tensor_tensor(dst[:, CTX:], tab[:, j, e0 * GRID:e0 * GRID + NA_KEYS], masks[:, kind, :], ALU.add)

        units = ctx_units + [(CTX // P + t, [(0, CTX), (CTX + na_first(t) * GRID, NA_KEYS)]) for t in range(SEQ // P)]
        Attention(core, 2, TOK2, TOK2, units, lambda s, u, j, t: s.pb[:, u % 2, 0:s.widths(u)], na_loads,
                  lambda it, rows, q0, n: h[rows, 6:8, :].rearrange("p k t -> p (k t)")[:, ds(it * TOK2 + q0, n)],
                  big + len(NA_KINDS) * NA_KEYS + 2 * NA_SLOTS * GRID, [4, 5], pool_bias=na_bias,
                  once=[(masks.rearrange("p a b -> p (a b)"), a["na_masks"])])
        t0 = CTX if last else 0
        GateTiles(core, h, [(3 + j, proj[(18 + j) * P:(19 + j) * P, :]) for j in range(3)]
                  + [(6 + j, proj[(27 + j) * P:(28 + j) * P, :]) for j in range(2)], big, t0)
        T = TOK2 - t0
        splits = T3 if not last else [(0, 512), (512, 1024)]
        y = R(big, KT, T)
        Gemm(core, [kview(a["w_out_2"][l])], [(0, 0, KT)], [(0, KT, 0)],
             lambda k, n0, n1, t0=t0: h[:, k, t0 + n0:t0 + n1], splits, "keep", 4, R(big, KT * T)).close()
        xl = x[:, :, t0:TOK2]
        Residual(core, xl, y, mod, [(0, 0, T)] if last else [(1, 0, CTX), (0, CTX, TOK2)])
        Norm(core, xl, xl, lambda k, par=par: par("ln_g", k), T, R(big, 4, T), "write", LN_EPS,
             b=lambda k, par=par: par("ln_b", k), center=True)
    StoreTokens(core, x, CTX, SEQ // P, a["out"], R(big, 2, D))


def rope_tables():
    t = np.arange(SEQ)
    inv = 10000.0 ** (-np.arange(16, dtype=np.float32) / 16)
    row, col = (t // GRID).astype(np.float32), (t % GRID).astype(np.float32)
    ar, ac = row[:, None] * inv, col[:, None] * inv
    ang = np.concatenate([ar, ar, ac, ac], 1).astype(np.float32)
    return [np.ascontiguousarray(np.tile(f(ang).T, (2, 1)).astype(np.float32)) for f in (np.cos, np.sin)]


def pack2(i):
    out = np.zeros((P, 2, NPAR2), np.float32)
    for l in range(2):
        def put(name, cols):
            out[:, l, PARAM2[name][0]:PARAM2[name][0] + PARAM2[name][1]] = cols

        put("b_mod", tiles(i["b_mod_2"][l]))
        put("rwkv_conv", tiles(i["rwkv_conv_2"][l]))
        put("decay_w0", tiles(i["decay_w0_2"][l]))
        put("iclr_a0", tiles(i["iclr_a0_2"][l]))
        for n in ("k_k", "k_a", "gn_g", "gn_b"):
            put(n, tiles(i[f"rwkv_{n}_2"][l]))
        put("r_k", tiles(i["rwkv_r_k_2"][l]))
        put("q_norm", np.tile(i["gqa_q_norm_2"][l], 2)[:, None])
        put("k_norm", np.tile(i["gqa_k_norm_2"][l], 2)[:, None])
        put("ln_g", tiles(i["ln_g_2"][l]))
        put("ln_b", tiles(i["ln_b_2"][l]))
    return out


def arrays2(i):
    low = np.zeros((2, P, 4, 384), np.float32)
    for d in range(2):
        low[:, 32 * d:32 * d + 32, d] = i["decay_w2_2"][:, d]
        low[:, 64 + 32 * d:96 + 32 * d, 2 + d] = i["iclr_a2_2"][:, d]
    pad = np.zeros((2, 4, 19, 127), np.float32)
    pad[:, :, 2:17, 48:79] = i["na_rpb_2"]
    cos, sin = rope_tables()
    cond = np.stack([tiles(i["c_2"][0]), tiles(i["c_ctx_2"])], 2)
    return {"params2": pack2(i), "cond": cond, "ctx_2": i["ctx_2"][0], "w_mod_2": i["w_mod_2"], "w_in_2": i["w_in_2"],
            "w_out_2": i["w_out_2"], "lowrank": low.reshape(2, P, 4 * 384), "rpb_pad": pad.reshape(2, 4, NA_TAB),
            "rope_cos": cos, "rope_sin": sin, "na_masks": na_masks()}


def program(nc, a, upto=999, first=0):
    with ExitStack() as ctx:
        core = Core(nc, ctx, a)
        R = core.region
        at = core.free0
        par = R(at, NPAR)
        at += NPAR
        par_end = at
        pcol = lambda name, i=0, n=1: par[:, PARAM[name][0] + i:PARAM[name][0] + i + n]
        xT = R(at, KT, SEQ)
        hT = R(at + KT * SEQ, KT, SEQ)
        big = at + 2 * KT * SEQ
        proj = nc.dram_tensor("proj1", (28 * P, SEQ), F32, kind="Internal").ap()
        kview = lambda w: w.rearrange("(k p) f -> p k f", p=P)
        two = [(0, 512), (512, 1024)]

        LoadInputs(core, [(core.C, a["consts"]), (par, a["params"])])
        LoadTokens(core, a["x"], SEQ // P, xT, 0, R(big, 2, D))
        tmp = R(big, 4, SEQ)
        Norm(core, xT, hT, lambda k: pcol("g_mix_pre", k), SEQ, tmp, "write", EPS)
        w_in = kview(a["w_in"])
        Gemm(core, [w_in], [(0, 0, KT)], [(0, 16, 0), (16 * P + 8, 12, 16)], lambda k, n0, n1: hT[:, k, n0:n1], two,
             "store", 4, proj, R(big, 4, SEQ)).close()
        beta, g = R(big, 32), R(big + 32, 32)
        GdnGates(core, hT, w_in[:, :, 16 * P:16 * P + 8], pcol("gates", 0, 8), beta, g, R(big + 64, 224))
        qkv = [R(big + 64 + i * GH * SEQ, GH * SEQ) for i in range(3)]
        rest = big + 64 + 3 * GH * SEQ
        mixT = hT
        GdnPrep(core, proj, pcol("conv_w", 0, 48), qkv, R(rest, 8300))
        Gdn(core, *qkv, beta, g, mixT, R(rest, 25 * 512 + 24))
        GdnOut(core, mixT, proj[12 * P:16 * P, :], pcol("onorm_g"), R(big, 4 * SEQ))
        flat = nc.dram_tensor("bias_flat", (BH, GELEN), F32, kind="Internal").ap()
        band = nc.dram_tensor("bias_band", (BH * P * GELEN,), F32, kind="Internal").ap()
        DilatedBias(core, a["rel_bias"], a["dilated"], flat, band.rearrange("(h p i) -> h p i", h=BH, p=P), R(big, 8 + 2 * GELEN))
        bias = R(big, 2, SEQ)

        def loads(it, s):
            row = lambda x: proj[ds(it * P + (16 + x) * P, P), 0:SEQ]
            shifted = lambda j: bass.AP(band.tensor, it * (2 * P * GELEN) + (j * P * GELEN + P - 1), [[GELEN - 1, P], [1, SEQ]])
            return [(s.q, row(0)), (s.k, row(4)), (s.v, row(8)), (bias[:, 0, :], shifted(0)), (bias[:, 1, :], shifted(1))]

        units = [(t, [(0, (t + 1) * P)]) for t in range(SEQ // P)]
        Attention(core, BH // 2, SEQ, SEQ, units, lambda s, u, j, t: bias[:, j, SEQ - (t + 1) * P:SEQ], loads,
                  lambda it, rows, q0, n: mixT[rows, 4:8, :].rearrange("p k t -> p (k t)")[:, ds(it * SEQ + q0, n)],
                  big + 2 * SEQ, [4, 5])
        y = R(big, KT, SEQ)
        tmp = R(big + KT * SEQ, 4, SEQ)
        Gemm(core, [kview(a["w_out"])], [(0, 0, KT)], [(0, KT, 0)], lambda k, n0, n1: mixT[:, k, n0:n1], two, "keep", 4,
             R(big, KT * SEQ)).close()
        Norm(core, y, xT, lambda k: pcol("g_mix_post", k), SEQ, tmp, "add", EPS)
        Norm(core, xT, hT, lambda k: pcol("g_ffn_pre", k), SEQ, tmp, "write", EPS)
        act = R(big, FFT, SEQ)
        Gemm(core, [kview(a["w_gate"]), kview(a["w_up"])], [(0, 0, KT), (1, 0, KT)], [(0, FFT, 0)],
             lambda k, n0, n1: hT[:, k, n0:n1], two, "gated", 4, R(big, FFT * SEQ), R(big + FFT * SEQ, 2, 512)).close()
        y = hT
        Gemm(core, [kview(a["w_down"])], [(0, 0, 8), (0, 8, 16), (0, 16, FFT)], [(0, KT, 0)],
             lambda k, n0, n1: act[:, k, n0:n1], two, "keep", 2, y.rearrange("p k t -> p (k t)")).close()
        Norm(core, y, xT, lambda k: pcol("g_ffn_post", k), SEQ, tmp, "add", EPS)
        second_block(nc, core, a, par_end, xT)
        core.stages = core.stages[first:upto]
        emit(nc, core)


def emit(nc, core):
    with nc.Block() as block:
        @block.sync
        def _(sp):
            for stage in core.stages:
                stage.sp(sp)

        @block.tensor
        def _(pe):
            pe.nop().then_inc(core.pe.sem, CREDIT)
            for stage in core.stages:
                stage.run_pe(pe)
                stage.finish(pe)

        @block.scalar
        def _(act):
            act.nop().then_inc(core.act.sem, CREDIT)
            for stage in core.stages:
                stage.run_act(act)
                stage.finish(act)

        @block.vector
        def _(dve):
            dve.nop().then_inc(core.dve.sem, CREDIT)
            for stage in core.stages:
                stage.run_dve(dve)
                stage.finish(dve)

        @block.gpsimd
        def _(pool):
            pool.nop().then_inc(core.pool.sem, CREDIT)
            for stage in core.stages:
                stage.run_pool(pool)
                stage.finish(pool)


def tiles(v):
    return np.asarray(v).reshape(-1, P).T


def pack1(i):
    out = np.zeros((P, NPAR), np.float32)

    def put(name, cols):
        out[:, PARAM[name][0]:PARAM[name][0] + PARAM[name][1]] = cols

    for n in ("g_mix_pre", "g_mix_post", "g_ffn_pre", "g_ffn_post"):
        put(n, tiles(i[n][0]))
    put("conv_w", i["conv_w"][0].reshape(4, 12, P).transpose(2, 1, 0).reshape(P, 48))
    put("onorm_g", i["onorm_g"][0][:, None])
    put("gates", np.concatenate([np.broadcast_to(i["a_log"][0], (P, 4)), np.broadcast_to(i["dt_bias"][0], (P, 4))], 1))
    return out


def arrays_of(i):
    return {**arrays2(i), "x": i["x"][0], "w_in": i["w_in"][0], "w_out": i["w_out"][0], "w_gate": i["w_gate"][0], "w_up": i["w_up"][0],
            "w_down": i["w_down"][0], "consts": constants(), "params": pack1(i), "dilated": dilated_table(),
            "rel_bias": np.concatenate([i["rel_bias"], np.ones((1, BH), np.float32)], 0)}


def kernel(**inputs):
    import concourse.bacc as bacc
    from concourse.bass_utils import run_bass_kernel_spmd

    nc = bacc.Bacc("TRN2", target_bir_lowering=False, num_devices=1)
    arrays = {n: np.ascontiguousarray(v) for n, v in arrays_of({n: np.asarray(v) for n, v in inputs.items()}).items()}
    aps = {n: nc.dram_tensor(n, v.shape, mybir.dt.from_np(v.dtype), kind="ExternalInput").ap() for n, v in arrays.items()}
    aps["out"] = nc.dram_tensor("out", (SEQ, D), F32, kind="ExternalOutput").ap()
    program(nc, aps)
    r = run_bass_kernel_spmd(nc, [arrays], core_ids=[0])
    return np.asarray(r.results[0]["out"]).reshape(1, SEQ, D)
```
